# Optimizing a Trainium2 kernel written in Bass

```python
import math
import jax, jax.numpy as jnp
from jax import lax
import numpy as np
import jax
import jax.numpy as jnp

D_MODEL = 1024
BATCH = 1
SEQ = 512
DEPTH = 2

HEAD_DIM = 64
ROPE_THETA = 500000.0
ROPE_FRAC = 4
EPS = 1e-6
Q_BLOCK = 128

A_WIDTH = D_MODEL // 2
A_GROUPS = 4
A_GDIM = A_WIDTH // A_GROUPS
A_CHUNK = 128

B_HEADS = 8
B_QK_DIM = 32
B_V_DIM = 2 * B_QK_DIM
B_WIDTH = B_HEADS * B_V_DIM

C_WIDTH = D_MODEL // 2
C_KERNEL = 31

D_HEADS = 8
D_KV_GROUPS = 2
D_WIDTH = D_HEADS * HEAD_DIM
CMP_BLOCK = 32
CMP_STRIDE = 16
CMP_HIDDEN = 2 * HEAD_DIM
SLC_BLOCK = 64
SLC_TOPK = 16
WINDOW = 512

MEM_TOKENS = 256
M_HEADS = 4
M_WIDTH = M_HEADS * HEAD_DIM

MIX_WIDTH = A_WIDTH + B_WIDTH + M_WIDTH
EVEN_SPLITS = (A_WIDTH, A_WIDTH, A_WIDTH,
               2 * B_HEADS * B_QK_DIM, 2 * B_HEADS * B_QK_DIM, B_WIDTH, B_WIDTH,
               M_WIDTH, M_WIDTH)
ODD_SPLITS = (C_WIDTH, C_WIDTH, C_WIDTH,
              D_WIDTH, 6 * D_KV_GROUPS * HEAD_DIM, 3 * D_HEADS, D_WIDTH,
              M_WIDTH, M_WIDTH)
EVEN_IN = sum(EVEN_SPLITS)
ODD_IN = sum(ODD_SPLITS)


def rms_norm(x, g):
    xf = x.astype(jnp.float32)
    y = xf * lax.rsqrt(jnp.mean(xf * xf, axis=-1, keepdims=True) + EPS)
    return (y * g.astype(jnp.float32)).astype(x.dtype)

def rope_partial(x, pos):
    d = x.shape[-1]
    rd = d // ROPE_FRAC
    half = rd // 2
    inv = ROPE_THETA ** (-jnp.arange(half, dtype=jnp.float32) / half)
    ang = pos.astype(jnp.float32)[:, None] * inv[None, :]
    cos = jnp.cos(ang).astype(x.dtype)
    sin = jnp.sin(ang).astype(x.dtype)
    x1, x2, rest = x[..., :half], x[..., half:rd], x[..., rd:]
    return jnp.concatenate([x1 * cos - x2 * sin, x1 * sin + x2 * cos, rest], axis=-1)

def masked_softmax(s, mask):
    s = jnp.where(mask, s, -jnp.inf)
    m = jnp.max(s, axis=-1, keepdims=True)
    m = jnp.where(jnp.isfinite(m), m, 0.0)
    e = jnp.where(mask, jnp.exp(s - m), 0.0)
    return e / jnp.maximum(jnp.sum(e, axis=-1, keepdims=True), jnp.finfo(jnp.float32).tiny)

def split_cols(x, sizes):
    return jnp.split(x, [int(v) for v in np.cumsum(sizes)[:-1]], axis=-1)

def chunked_sgu(u, v, w_s, b_s, v_gain):
    Bz, S, _ = v.shape
    v = rms_norm(v.reshape(Bz, S, A_GROUPS, A_GDIM), v_gain.reshape(A_GROUPS, A_GDIM))
    v = v.reshape(Bz, S // A_CHUNK, A_CHUNK, A_GROUPS, A_GDIM)
    causal = jnp.tril(jnp.ones((A_CHUNK, A_CHUNK), dtype=bool))
    w = jnp.where(causal[None], w_s, 0.0)
    z = jnp.einsum('gts,bcsgd->bctgd', w, v) + b_s.T[:, :, None]
    return u * z.reshape(Bz, S, A_WIDTH)

def diff_attention(q, k, v, lam):
    Bz, H, _, S, dk = q.shape
    dv = v.shape[-1]
    nblk = S // Q_BLOCK
    scale = dk ** -0.5
    kpos = jnp.arange(S)
    qb = q.reshape(Bz, H, 2, nblk, Q_BLOCK, dk).transpose(3, 0, 1, 2, 4, 5)

    def block(args):
        qi, c = args
        qpos = c * Q_BLOCK + jnp.arange(Q_BLOCK)
        s = jnp.einsum('bhmqd,bhmkd->bhmqk', qi, k).astype(jnp.float32) * scale
        s = jnp.where(kpos[None, :] <= qpos[:, None], s, -jnp.inf)
        p = jax.nn.softmax(s, axis=-1)
        pd = p[:, :, 0] - lam * p[:, :, 1]
        return jnp.einsum('bhqk,bhkd->bhqd', pd.astype(v.dtype), v)

    o = lax.map(block, (qb, jnp.arange(nblk)))
    return o.transpose(1, 0, 3, 2, 4).reshape(Bz, S, H, dv)

def memory_attention(q, mem_n, w_kv, qnorm, knorm):
    Bz, S, _ = q.shape
    k, v = jnp.split(mem_n @ w_kv, 2, axis=-1)
    q = rms_norm(q.reshape(Bz, S, M_HEADS, HEAD_DIM), qnorm)
    k = rms_norm(k.reshape(Bz, -1, M_HEADS, HEAD_DIM), knorm)
    v = v.reshape(Bz, -1, M_HEADS, HEAD_DIM)
    s = jnp.einsum('bshd,bmhd->bhsm', q, k).astype(jnp.float32) * (HEAD_DIM ** -0.5)
    p = jax.nn.softmax(s, axis=-1)
    return jnp.einsum('bhsm,bmhd->bshd', p.astype(v.dtype), v).reshape(Bz, S, M_WIDTH)

def conformer_conv(a, b, conv_w, conv_b, norm_g):
    h = a * jax.nn.sigmoid(b)
    hp = jnp.pad(h, ((0, 0), (C_KERNEL - 1, 0), (0, 0)))
    y = lax.conv_general_dilated(hp, conv_w[:, None, :], window_strides=(1,), padding='VALID',
                                 dimension_numbers=('NWC', 'WIO', 'NWC'),
                                 feature_group_count=C_WIDTH) + conv_b
    return jax.nn.silu(rms_norm(y, norm_g))

def compress(t, cmp_idx, pos_emb, w1, w2):
    Bz, _, G, hd = t.shape
    blocks = t[:, cmp_idx] + pos_emb[:, None, :]
    flat = blocks.transpose(0, 1, 3, 2, 4).reshape(Bz, cmp_idx.shape[0], G, CMP_BLOCK * hd)
    return jax.nn.silu(flat @ w1) @ w2

def cmp_to_slc_overlap(n_cmp, n_slc):
    start = np.arange(n_cmp) * CMP_STRIDE
    s0 = np.arange(n_slc) * SLC_BLOCK
    lo = np.maximum(start[:, None], s0[None, :])
    hi = np.minimum(start[:, None] + CMP_BLOCK, s0[None, :] + SLC_BLOCK)
    return (np.clip(hi - lo, 0, None) / CMP_BLOCK).astype(np.float32)

def nsa(q, kv, gates, pos, qnorm, knorm, cmp_pos_k, cmp_w1_k, cmp_w2_k,
        cmp_pos_v, cmp_w1_v, cmp_w2_v):
    Bz, S = q.shape[:2]
    G, R, hd = D_KV_GROUPS, D_HEADS // D_KV_GROUPS, HEAD_DIM
    nblk = S // Q_BLOCK
    n_cmp = (S - CMP_BLOCK) // CMP_STRIDE + 1
    n_slc = S // SLC_BLOCK
    n_sel = min(SLC_TOPK, n_slc)
    scale = hd ** -0.5

    q = rope_partial(rms_norm(q, qnorm).transpose(0, 2, 1, 3), pos).reshape(Bz, G, R, S, hd)
    k_cmp_raw, v_cmp_raw, k_slc, v_slc, k_win, v_win = [kv[:, :, i] for i in range(6)]

    cmp_idx = np.arange(n_cmp)[:, None] * CMP_STRIDE + np.arange(CMP_BLOCK)[None, :]
    cmp_end = jnp.asarray(cmp_idx[:, -1])
    kc = compress(k_cmp_raw, cmp_idx, cmp_pos_k, cmp_w1_k, cmp_w2_k)
    vc = compress(v_cmp_raw, cmp_idx, cmp_pos_v, cmp_w1_v, cmp_w2_v).transpose(0, 2, 1, 3)
    kc = rope_partial(rms_norm(kc, knorm).transpose(0, 2, 1, 3), cmp_end)

    ks = rope_partial(rms_norm(k_slc, knorm).transpose(0, 2, 1, 3), pos)
    kb = ks.reshape(Bz, G, n_slc, SLC_BLOCK, hd)
    vb = v_slc.transpose(0, 2, 1, 3).reshape(Bz, G, n_slc, SLC_BLOCK, hd)

    pad = ((0, 0), (0, 0), (WINDOW, 0), (0, 0))
    kw = jnp.pad(rope_partial(rms_norm(k_win, knorm).transpose(0, 2, 1, 3), pos), pad)
    vw = jnp.pad(v_win.transpose(0, 2, 1, 3), pad)

    overlap = jnp.asarray(cmp_to_slc_overlap(n_cmp, n_slc))
    b_ix = jnp.arange(Bz)[:, None, None, None]
    g_ix = jnp.arange(G)[None, :, None, None]
    blk_tok = jnp.arange(SLC_BLOCK)
    slc_ids = jnp.arange(n_slc)
    win_off = jnp.arange(WINDOW + Q_BLOCK) - WINDOW

    qb = q.reshape(Bz, G, R, nblk, Q_BLOCK, hd).transpose(3, 0, 1, 2, 4, 5)
    gb = gates.transpose(0, 2, 1, 3).reshape(Bz, G, R, nblk, Q_BLOCK, 3).transpose(3, 0, 1, 2, 4, 5)

    def block(args):
        qi, gt, c = args
        qpos = c * Q_BLOCK + jnp.arange(Q_BLOCK)
        s = jnp.einsum('bgrqd,bgnd->bgrqn', qi, kc).astype(jnp.float32) * scale
        p_c = masked_softmax(s, cmp_end[None, :] <= qpos[:, None])
        o_c = jnp.einsum('bgrqn,bgnd->bgrqd', p_c.astype(vc.dtype), vc)
        imp = jnp.einsum('bgrqn,nj->bgqj', p_c, overlap)
        cur = (qpos // SLC_BLOCK)[:, None]
        imp = jnp.where(slc_ids[None, :] > cur, -jnp.inf, imp)
        forced = (slc_ids[None, :] == 0) | (slc_ids[None, :] == cur) | (slc_ids[None, :] == cur - 1)
        imp = jnp.where(forced, jnp.inf, imp)
        _, sel = lax.top_k(imp, n_sel)
        ksel = kb[b_ix, g_ix, sel].reshape(Bz, G, Q_BLOCK, n_sel * SLC_BLOCK, hd)
        vsel = vb[b_ix, g_ix, sel].reshape(Bz, G, Q_BLOCK, n_sel * SLC_BLOCK, hd)
        kpos = (sel[..., None] * SLC_BLOCK + blk_tok).reshape(Bz, G, Q_BLOCK, n_sel * SLC_BLOCK)
        s = jnp.einsum('bgrqd,bgqkd->bgrqk', qi, ksel).astype(jnp.float32) * scale
        p_s = masked_softmax(s, (kpos <= qpos[:, None])[:, :, None])
        o_s = jnp.einsum('bgrqk,bgqkd->bgrqd', p_s.astype(vsel.dtype), vsel)
        kwi = lax.dynamic_slice_in_dim(kw, c * Q_BLOCK, WINDOW + Q_BLOCK, axis=2)
        vwi = lax.dynamic_slice_in_dim(vw, c * Q_BLOCK, WINDOW + Q_BLOCK, axis=2)
        wpos = c * Q_BLOCK + win_off
        dpos = qpos[:, None] - wpos[None, :]
        s = jnp.einsum('bgrqd,bgkd->bgrqk', qi, kwi).astype(jnp.float32) * scale
        p_w = masked_softmax(s, (wpos[None, :] >= 0) & (dpos >= 0) & (dpos < WINDOW))
        o_w = jnp.einsum('bgrqk,bgkd->bgrqd', p_w.astype(vwi.dtype), vwi)
        return gt[..., 0:1] * o_c + gt[..., 1:2] * o_s + gt[..., 2:3] * o_w

    o = lax.map(block, (qb, gb, jnp.arange(nblk)))
    return o.transpose(1, 0, 4, 2, 3, 5).reshape(Bz, S, D_WIDTH)

def even_layer(x, mem_n, pos, layer, norm_g, w_in, a_vnorm, a_ws, a_bs, b_qnorm, b_knorm,
               b_lq1, b_lk1, b_lq2, b_lk2, b_subln, m_wkv, m_qnorm, m_knorm, w_out):
    Bz, S, _ = x.shape
    h = rms_norm(x, norm_g)
    a_u, a_v, a_g, b_q, b_k, b_v, b_g, m_q, m_g = split_cols(h @ w_in, EVEN_SPLITS)
    y_a = chunked_sgu(jax.nn.gelu(a_u), jax.nn.gelu(a_v), a_ws, a_bs, a_vnorm) * jax.nn.silu(a_g)
    lam_init = 0.8 - 0.6 * math.exp(-0.3 * layer)
    lam = (jnp.exp(jnp.sum(b_lq1.astype(jnp.float32) * b_lk1.astype(jnp.float32)))
           - jnp.exp(jnp.sum(b_lq2.astype(jnp.float32) * b_lk2.astype(jnp.float32))) + lam_init)
    q = rms_norm(b_q.reshape(Bz, S, B_HEADS, 2, B_QK_DIM), b_qnorm).transpose(0, 2, 3, 1, 4)
    k = rms_norm(b_k.reshape(Bz, S, B_HEADS, 2, B_QK_DIM), b_knorm).transpose(0, 2, 3, 1, 4)
    q, k = rope_partial(q, pos), rope_partial(k, pos)
    v = b_v.reshape(Bz, S, B_HEADS, B_V_DIM).transpose(0, 2, 1, 3)
    o_b = rms_norm(diff_attention(q, k, v, lam), b_subln) * (1.0 - lam_init)
    y_b = o_b.reshape(Bz, S, B_WIDTH) * jax.nn.silu(b_g)
    y_m = memory_attention(m_q, mem_n, m_wkv, m_qnorm, m_knorm) * jax.nn.silu(m_g)
    return x + jnp.concatenate([y_a, y_b, y_m], axis=-1) @ w_out

def odd_layer(x, mem_n, pos, norm_g, w_in, c_conv_w, c_conv_b, c_norm, d_qnorm, d_knorm,
              cmp_pos_k, cmp_w1_k, cmp_w2_k, cmp_pos_v, cmp_w1_v, cmp_w2_v,
              m_wkv, m_qnorm, m_knorm, w_out):
    Bz, S, _ = x.shape
    h = rms_norm(x, norm_g)
    c_a, c_b, c_g, d_q, d_kv, d_bg, d_g, m_q, m_g = split_cols(h @ w_in, ODD_SPLITS)
    y_c = conformer_conv(c_a, c_b, c_conv_w, c_conv_b, c_norm) * jax.nn.silu(c_g)
    kv = d_kv.reshape(Bz, S, 6, D_KV_GROUPS, HEAD_DIM)
    gates = jax.nn.sigmoid(d_bg.reshape(Bz, S, D_HEADS, 3))
    y_d = nsa(d_q.reshape(Bz, S, D_HEADS, HEAD_DIM), kv, gates, pos, d_qnorm, d_knorm,
              cmp_pos_k, cmp_w1_k, cmp_w2_k, cmp_pos_v, cmp_w1_v, cmp_w2_v) * jax.nn.silu(d_g)
    y_m = memory_attention(m_q, mem_n, m_wkv, m_qnorm, m_knorm) * jax.nn.silu(m_g)
    return x + jnp.concatenate([y_c, y_d, y_m], axis=-1) @ w_out

def first_inputs(seed: int = 0) -> dict:
    key = jax.random.key(seed)
    keys = iter(jax.random.split(key, 48))

    def nrm(shape, scale):
        return jax.random.normal(next(keys), shape, jnp.float32) * scale

    def gain(n):
        return 1.0 + nrm((n,), 0.05)

    return {
        "x": nrm((BATCH, SEQ, D_MODEL), 1.0),
        "mem": nrm((BATCH, MEM_TOKENS, D_MODEL), 1.0),
        "mem_norm": gain(D_MODEL),
        "l0_norm": gain(D_MODEL),
        "l0_w_in": nrm((D_MODEL, EVEN_IN), D_MODEL ** -0.5),
        "l0_a_vnorm": gain(A_WIDTH),
        "l0_a_ws": nrm((A_GROUPS, A_CHUNK, A_CHUNK), A_CHUNK ** -0.5),
        "l0_a_bs": 1.0 + nrm((A_GROUPS, A_CHUNK), 0.1),
        "l0_b_qnorm": gain(B_QK_DIM),
        "l0_b_knorm": gain(B_QK_DIM),
        "l0_b_lq1": nrm((B_QK_DIM,), 0.1),
        "l0_b_lk1": nrm((B_QK_DIM,), 0.1),
        "l0_b_lq2": nrm((B_QK_DIM,), 0.1),
        "l0_b_lk2": nrm((B_QK_DIM,), 0.1),
        "l0_b_subln": gain(B_V_DIM),
        "l0_m_wkv": nrm((D_MODEL, 2 * M_WIDTH), D_MODEL ** -0.5),
        "l0_m_qnorm": gain(HEAD_DIM),
        "l0_m_knorm": gain(HEAD_DIM),
        "l0_w_out": nrm((MIX_WIDTH, D_MODEL), MIX_WIDTH ** -0.5),
        "l1_norm": gain(D_MODEL),
        "l1_w_in": nrm((D_MODEL, ODD_IN), D_MODEL ** -0.5),
        "l1_c_conv_w": nrm((C_KERNEL, C_WIDTH), C_KERNEL ** -0.5),
        "l1_c_conv_b": nrm((C_WIDTH,), 0.02),
        "l1_c_norm": gain(C_WIDTH),
        "l1_d_qnorm": gain(HEAD_DIM),
        "l1_d_knorm": gain(HEAD_DIM),
        "l1_d_cmp_pos_k": nrm((CMP_BLOCK, HEAD_DIM), 0.02),
        "l1_d_cmp_w1_k": nrm((CMP_BLOCK * HEAD_DIM, CMP_HIDDEN), (CMP_BLOCK * HEAD_DIM) ** -0.5),
        "l1_d_cmp_w2_k": nrm((CMP_HIDDEN, HEAD_DIM), CMP_HIDDEN ** -0.5),
        "l1_d_cmp_pos_v": nrm((CMP_BLOCK, HEAD_DIM), 0.02),
        "l1_d_cmp_w1_v": nrm((CMP_BLOCK * HEAD_DIM, CMP_HIDDEN), (CMP_BLOCK * HEAD_DIM) ** -0.5),
        "l1_d_cmp_w2_v": nrm((CMP_HIDDEN, HEAD_DIM), CMP_HIDDEN ** -0.5),
        "l1_m_wkv": nrm((D_MODEL, 2 * M_WIDTH), D_MODEL ** -0.5),
        "l1_m_qnorm": gain(HEAD_DIM),
        "l1_m_knorm": gain(HEAD_DIM),
        "l1_w_out": nrm((MIX_WIDTH, D_MODEL), MIX_WIDTH ** -0.5),
    }

def first_block(x, mem, mem_norm,
              l0_norm, l0_w_in, l0_a_vnorm, l0_a_ws, l0_a_bs, l0_b_qnorm, l0_b_knorm,
              l0_b_lq1, l0_b_lk1, l0_b_lq2, l0_b_lk2, l0_b_subln, l0_m_wkv, l0_m_qnorm,
              l0_m_knorm, l0_w_out,
              l1_norm, l1_w_in, l1_c_conv_w, l1_c_conv_b, l1_c_norm, l1_d_qnorm, l1_d_knorm,
              l1_d_cmp_pos_k, l1_d_cmp_w1_k, l1_d_cmp_w2_k, l1_d_cmp_pos_v, l1_d_cmp_w1_v,
              l1_d_cmp_w2_v, l1_m_wkv, l1_m_qnorm, l1_m_knorm, l1_w_out):
    pos = jnp.arange(x.shape[1], dtype=jnp.int32)
    mem_n = rms_norm(mem, mem_norm)
    even_params = (l0_norm, l0_w_in, l0_a_vnorm, l0_a_ws, l0_a_bs, l0_b_qnorm, l0_b_knorm,
                   l0_b_lq1, l0_b_lk1, l0_b_lq2, l0_b_lk2, l0_b_subln, l0_m_wkv, l0_m_qnorm,
                   l0_m_knorm, l0_w_out)
    odd_params = (l1_norm, l1_w_in, l1_c_conv_w, l1_c_conv_b, l1_c_norm, l1_d_qnorm, l1_d_knorm,
                  l1_d_cmp_pos_k, l1_d_cmp_w1_k, l1_d_cmp_w2_k, l1_d_cmp_pos_v, l1_d_cmp_w1_v,
                  l1_d_cmp_w2_v, l1_m_wkv, l1_m_qnorm, l1_m_knorm, l1_w_out)
    for layer in range(DEPTH):
        if layer % 2 == 0:
            x = even_layer(x, mem_n, pos, layer + 1, *even_params)
        else:
            x = odd_layer(x, mem_n, pos, *odd_params)
    return x


DEPTH_2 = 1

CTX_LEN = 256
GRID_W = 64
N_BRANCHES = 2
F32 = jnp.float32

DN_HEADS = 8
DN_DK = 128
DN_DV = 128
DN_CONV = 5
DN_CHUNK = 64
MLA_HEADS = 8
MLA_Q_RANK = 384
MLA_KV_RANK = 256
MLA_NOPE = 128
MLA_ROPE = 64
MLA_QK_DIM = MLA_NOPE + MLA_ROPE
MLA_V = 128
ROPE_BASE = 10000.0
N_EXPERTS = 16
EC_CAPACITY = 2
EXPERT_FF = 1408

DN_QKV_DIM = 2 * DN_HEADS * DN_DK + DN_HEADS * DN_DV
OFF_Z = DN_QKV_DIM
OFF_ALPHA = OFF_Z + DN_HEADS * DN_DV
OFF_BETA = OFF_ALPHA + 2 * DN_HEADS
OFF_CQ = OFF_BETA + 2 * DN_HEADS
OFF_CKV = OFF_CQ + MLA_Q_RANK
OFF_KROPE = OFF_CKV + MLA_KV_RANK
OFF_GATE = OFF_KROPE + MLA_ROPE
D_IN = OFF_GATE + N_BRANCHES * D_MODEL
IN_OFFSETS = (OFF_Z, OFF_ALPHA, OFF_BETA, OFF_CQ, OFF_CKV, OFF_KROPE, OFF_GATE)


def rms_norm_2(x, g):
    xf = x.astype(F32)
    y = xf * lax.rsqrt(jnp.mean(xf * xf, axis=-1, keepdims=True) + EPS)
    return y.astype(x.dtype) * g

def l2_norm(x):
    return x * lax.rsqrt(jnp.sum(x * x, axis=-1, keepdims=True) + EPS)

def adaln(cond, ada_w, ada_b):
    mod = jax.nn.silu(cond) @ ada_w + ada_b
    return jnp.split(mod[:, None, :], 6, axis=-1)

def modulate(x, g, shift, scale):
    return rms_norm_2(x, g) * (1.0 + scale) + shift

def short_conv(x, w):
    pad = DN_CONV // 2
    y = lax.conv_general_dilated(x, w[:, None, :], window_strides=(1,), padding=[(pad, pad)],
                                 dimension_numbers=('NWC', 'WIO', 'NWC'), feature_group_count=x.shape[-1])
    return jax.nn.silu(y)

def gated_delta_chunked(q, k, v, g, beta, s0):
    b_, n_tok, n_h, dk = q.shape
    dv = v.shape[-1]
    n_chunk = n_tok // DN_CHUNK

    def to_chunks(t):
        return jnp.moveaxis(t.reshape(b_, n_chunk, DN_CHUNK, n_h, *t.shape[3:]), 3, 1)

    q, k, v, g, beta = (to_chunks(t) for t in (q, k, v, g, beta))
    q = q * dk ** -0.5
    g = jnp.cumsum(g, axis=-1)
    incl = jnp.tril(jnp.ones((DN_CHUNK, DN_CHUNK), dtype=bool))
    strict = jnp.tril(jnp.ones((DN_CHUNK, DN_CHUNK), dtype=bool), -1)
    decay = jnp.exp(jnp.where(incl, g[..., :, None] - g[..., None, :], -jnp.inf))
    k_beta = k * beta[..., None]
    m = jnp.where(strict, jnp.einsum('bhnid,bhnjd->bhnij', k_beta, k) * decay, 0.0)
    eye = jnp.eye(DN_CHUNK, dtype=q.dtype)
    t_inv = lax.linalg.triangular_solve(m + eye, jnp.broadcast_to(eye, m.shape), left_side=True,
                                        lower=True, unit_diagonal=True)
    u = jnp.einsum('bhnij,bhnjd->bhnid', t_inv, v * beta[..., None])
    w = jnp.einsum('bhnij,bhnjd->bhnid', t_inv, k_beta * jnp.exp(g)[..., None])
    qk = jnp.where(incl, jnp.einsum('bhnid,bhnjd->bhnij', q, k) * decay, 0.0)
    q_dec = q * jnp.exp(g)[..., None]
    k_dec = k * jnp.exp(g[..., -1:] - g)[..., None]
    chunk_decay = jnp.exp(g[..., -1])

    def chunk_step(s, xs):
        qk_c, q_c, k_c, u_c, w_c, a_c = xs
        v_new = u_c - jnp.einsum('bhik,bhkv->bhiv', w_c, s)
        o_c = jnp.einsum('bhik,bhkv->bhiv', q_c, s) + jnp.einsum('bhij,bhjv->bhiv', qk_c, v_new)
        s = s * a_c[..., None, None] + jnp.einsum('bhik,bhiv->bhkv', k_c, v_new)
        return s, o_c

    xs = tuple(jnp.moveaxis(t, 2, 0) for t in (qk, q_dec, k_dec, u, w, chunk_decay))
    s_final, o = lax.scan(chunk_step, s0, xs)
    o = jnp.transpose(o, (1, 0, 3, 2, 4)).reshape(b_, n_tok, n_h, dv)
    return o, s_final

def deltanet_inputs(qkv, alpha, beta_logit, conv_w, a_log, dt_bias):
    b_, n_tok, _ = qkv.shape
    qkv = short_conv(qkv, conv_w)
    q, k, v = jnp.split(qkv, [DN_HEADS * DN_DK, 2 * DN_HEADS * DN_DK], axis=-1)
    q = l2_norm(q.astype(F32).reshape(b_, n_tok, DN_HEADS, DN_DK))
    k = l2_norm(k.astype(F32).reshape(b_, n_tok, DN_HEADS, DN_DK))
    v = v.astype(F32).reshape(b_, n_tok, DN_HEADS, DN_DV)
    alpha = alpha.astype(F32).reshape(b_, n_tok, 2, DN_HEADS)
    g = -jnp.exp(a_log.astype(F32)) * jax.nn.softplus(alpha + dt_bias.astype(F32))
    beta = jax.nn.sigmoid(beta_logit.astype(F32).reshape(b_, n_tok, 2, DN_HEADS))
    return q, k, v, g, beta

def deltanet_bidir(q, k, v, g, beta, s0_fwd, s0_bwd):
    o_f, s_f = gated_delta_chunked(q, k, v, g[:, :, 0], beta[:, :, 0], s0_fwd)
    flip = lambda t: jnp.flip(t, axis=1)
    o_b, s_b = gated_delta_chunked(flip(q), flip(k), flip(v), flip(g[:, :, 1]), flip(beta[:, :, 1]), s0_bwd)
    return o_f + flip(o_b), s_f, s_b

def deltanet_out(o, z, norm_g):
    b_, n_tok = o.shape[:2]
    zf = z.astype(F32).reshape(b_, n_tok, DN_HEADS, DN_DV)
    y = rms_norm_2(o, norm_g.astype(F32)) * jax.nn.silu(zf)
    return y.reshape(b_, n_tok, DN_HEADS * DN_DV).astype(z.dtype)

def axial_rope_tables(rows, dtype):
    row = jnp.repeat(jnp.arange(rows), GRID_W).astype(F32)
    col = jnp.broadcast_to(jnp.arange(GRID_W), (rows, GRID_W)).reshape(-1).astype(F32)
    n_freq = MLA_ROPE // 4
    inv_freq = ROPE_BASE ** (-jnp.arange(n_freq, dtype=F32) / n_freq)
    ang_r = row[:, None] * inv_freq
    ang_c = col[:, None] * inv_freq
    ang = jnp.concatenate([ang_r, ang_r, ang_c, ang_c], axis=-1)[:, None, :]
    return jnp.cos(ang).astype(dtype), jnp.sin(ang).astype(dtype)

def apply_rope_tail(t, rope):
    cos, sin = rope
    nope, pe = jnp.split(t, [MLA_NOPE], axis=-1)
    x1, x2, x3, x4 = jnp.split(pe, 4, axis=-1)
    rot = jnp.concatenate([-x2, x1, -x4, x3], axis=-1)
    return jnp.concatenate([nope, pe * cos + rot * sin], axis=-1)

def mla_queries(c_q, q_a_norm_g, w_uq, q_norm_g, rope):
    b_, n_tok, _ = c_q.shape
    q = (rms_norm_2(c_q, q_a_norm_g) @ w_uq).reshape(b_, n_tok, MLA_HEADS, MLA_QK_DIM)
    q = rms_norm_2(q, q_norm_g)
    if rope is not None:
        q = apply_rope_tail(q, rope)
    return jnp.transpose(q, (0, 2, 1, 3))

def mla_keys_values(c_kv, k_rope, kv_a_norm_g, w_ukv, k_norm_g, rope):
    b_, n_tok, _ = c_kv.shape
    kv = (rms_norm_2(c_kv, kv_a_norm_g) @ w_ukv).reshape(b_, n_tok, MLA_HEADS, MLA_NOPE + MLA_V)
    k_nope, v = jnp.split(kv, [MLA_NOPE], axis=-1)
    k_pe = jnp.broadcast_to(k_rope[:, :, None, :], (b_, n_tok, MLA_HEADS, MLA_ROPE))
    k = rms_norm_2(jnp.concatenate([k_nope, k_pe], axis=-1), k_norm_g)
    if rope is not None:
        k = apply_rope_tail(k, rope)
    return jnp.transpose(k, (0, 2, 1, 3)), jnp.transpose(v, (0, 2, 1, 3))

def softmax_attention(q, k, v):
    b_, n_h, n_tok, dh = q.shape
    n_blk = n_tok // Q_BLOCK
    q_blocks = jnp.moveaxis(q.reshape(b_, n_h, n_blk, Q_BLOCK, dh), 2, 0)
    scale = dh ** -0.5

    def attend_block(qb):
        s = jnp.einsum('bhqd,bhkd->bhqk', qb, k, preferred_element_type=F32) * scale
        p = jax.nn.softmax(s, axis=-1).astype(v.dtype)
        return jnp.einsum('bhqk,bhkd->bhqd', p, v)

    o = lax.map(attend_block, q_blocks)
    o = jnp.moveaxis(o, 0, 2).reshape(b_, n_h, n_tok, -1)
    return jnp.transpose(o, (0, 2, 1, 3)).reshape(b_, n_tok, -1)

def merge_branches(y_a, y_b, gate_logits, w_out_a, w_out_b, w_o):
    g_a, g_b = jnp.split(jax.nn.sigmoid(gate_logits), N_BRANCHES, axis=-1)
    return (g_a * (y_a @ w_out_a) + g_b * (y_b @ w_out_b)) @ w_o

def expert_choice_moe(h, router_w, w_gate, w_up, w_down):
    b_, n_tok, d = h.shape
    cap = EC_CAPACITY * n_tok // N_EXPERTS
    affinity = jax.nn.softmax((h @ router_w).astype(F32), axis=-1)
    gate, idx = lax.top_k(jnp.swapaxes(affinity, 1, 2), cap)
    xe = jax.vmap(lambda hb, ib: hb[ib])(h, idx)
    hid = jax.nn.silu(jnp.einsum('becd,edf->becf', xe, w_gate)) * jnp.einsum('becd,edf->becf', xe, w_up)
    ye = jnp.einsum('becf,efd->becd', hid, w_down) * gate[..., None].astype(h.dtype)
    return jax.vmap(lambda ib, yb: jnp.zeros((n_tok, d), yb.dtype).at[ib.reshape(-1)].add(yb.reshape(-1, d)))(idx, ye)

def second_inputs(seed: int = 0) -> dict:
    key = jax.random.key(seed)
    ks = jax.random.split(key, 26)
    d = D_MODEL
    nrm = lambda k, shape, scale: jax.random.normal(k, shape, F32) * scale
    gain = lambda k, n: 1.0 + 0.02 * jax.random.normal(k, (DEPTH_2, n), F32)
    dt = jnp.exp(jax.random.uniform(ks[10], (DEPTH_2, 2, DN_HEADS), F32, math.log(1e-3), math.log(1e-1)))
    return {
        'x': nrm(ks[0], (BATCH, SEQ, d), 1.0),
        'c': nrm(ks[1], (BATCH, d), 1.0),
        'ctx': nrm(ks[2], (BATCH, CTX_LEN, d), 1.0),
        'c_ctx': nrm(ks[3], (d,), 1.0),
        'ada_w': nrm(ks[4], (DEPTH_2, d, 6 * d), d ** -0.5),
        'ada_b': nrm(ks[5], (DEPTH_2, 6 * d), 0.02),
        'norm1_g': gain(ks[6], d),
        'norm2_g': gain(ks[7], d),
        'w_in': nrm(ks[8], (DEPTH_2, d, D_IN), d ** -0.5),
        'conv_w': nrm(ks[9], (DEPTH_2, DN_CONV, DN_QKV_DIM), DN_CONV ** -0.5),
        'a_log': jnp.log(jax.random.uniform(ks[11], (DEPTH_2, 2, DN_HEADS), F32, 1.0, 16.0)),
        'dt_bias': dt + jnp.log(-jnp.expm1(-dt)),
        'dn_norm_g': gain(ks[12], DN_DV),
        'w_out_a': nrm(ks[13], (DEPTH_2, DN_HEADS * DN_DV, d), (DN_HEADS * DN_DV) ** -0.5),
        'q_a_norm_g': gain(ks[14], MLA_Q_RANK),
        'w_uq': nrm(ks[15], (DEPTH_2, MLA_Q_RANK, MLA_HEADS * MLA_QK_DIM), MLA_Q_RANK ** -0.5),
        'kv_a_norm_g': gain(ks[16], MLA_KV_RANK),
        'w_ukv': nrm(ks[17], (DEPTH_2, MLA_KV_RANK, MLA_HEADS * (MLA_NOPE + MLA_V)), MLA_KV_RANK ** -0.5),
        'q_norm_g': gain(ks[18], MLA_QK_DIM),
        'k_norm_g': gain(ks[19], MLA_QK_DIM),
        'w_out_b': nrm(ks[20], (DEPTH_2, MLA_HEADS * MLA_V, d), (MLA_HEADS * MLA_V) ** -0.5),
        'w_o': nrm(ks[21], (DEPTH_2, d, d), d ** -0.5),
        'router_w': nrm(ks[22], (DEPTH_2, d, N_EXPERTS), d ** -0.5),
        'w_gate': nrm(ks[23], (DEPTH_2, N_EXPERTS, d, EXPERT_FF), d ** -0.5),
        'w_up': nrm(ks[24], (DEPTH_2, N_EXPERTS, d, EXPERT_FF), d ** -0.5),
        'w_down': nrm(ks[25], (DEPTH_2, N_EXPERTS, EXPERT_FF, d), EXPERT_FF ** -0.5),
    }

def second_block(x, c, ctx, c_ctx, ada_w, ada_b, norm1_g, norm2_g, w_in, conv_w, a_log, dt_bias, dn_norm_g,
              w_out_a, q_a_norm_g, w_uq, kv_a_norm_g, w_ukv, q_norm_g, k_norm_g, w_out_b, w_o, router_w,
              w_gate, w_up, w_down):
    b_, n_lat, _ = x.shape
    rows = n_lat // GRID_W
    rope = axial_rope_tables(rows, x.dtype)
    zero_state = jnp.zeros((b_, DN_HEADS, DN_DK, DN_DV), F32)
    for i in range(DEPTH_2):
        last = i == DEPTH_2 - 1
        mod_x = adaln(c, ada_w[i], ada_b[i])
        mod_c = adaln(c_ctx[None], ada_w[i], ada_b[i])

        h_c = modulate(ctx, norm1_g[i], mod_c[0], mod_c[1])
        h_x = modulate(x, norm1_g[i], mod_x[0], mod_x[1])
        qkv_c, z_c, al_c, be_c, cq_c, ckv_c, kr_c, gt_c = jnp.split(h_c @ w_in[i], IN_OFFSETS, axis=-1)
        qkv_x, z_x, al_x, be_x, cq_x, ckv_x, kr_x, gt_x = jnp.split(h_x @ w_in[i], IN_OFFSETS, axis=-1)

        o_dn_c, s_fwd, s_bwd = deltanet_bidir(*deltanet_inputs(qkv_c, al_c, be_c, conv_w[i], a_log[i], dt_bias[i]),
                                              zero_state, zero_state)
        o_dn_x, _, _ = deltanet_bidir(*deltanet_inputs(qkv_x, al_x, be_x, conv_w[i], a_log[i], dt_bias[i]),
                                      s_fwd, s_bwd)

        k_c, v_c = mla_keys_values(ckv_c, kr_c, kv_a_norm_g[i], w_ukv[i], k_norm_g[i], None)
        k_x, v_x = mla_keys_values(ckv_x, kr_x, kv_a_norm_g[i], w_ukv[i], k_norm_g[i], rope)
        q_x = mla_queries(cq_x, q_a_norm_g[i], w_uq[i], q_norm_g[i], rope)
        o_mla_x = softmax_attention(q_x, jnp.concatenate([k_c, k_x], axis=2), jnp.concatenate([v_c, v_x], axis=2))

        mix_x = merge_branches(deltanet_out(o_dn_x, z_x, dn_norm_g[i]), o_mla_x, gt_x, w_out_a[i], w_out_b[i], w_o[i])
        x_mid = x + mod_x[2] * mix_x

        if not last:
            q_c = mla_queries(cq_c, q_a_norm_g[i], w_uq[i], q_norm_g[i], None)
            o_mla_c = softmax_attention(q_c, k_c, v_c)
            mix_c = merge_branches(deltanet_out(o_dn_c, z_c, dn_norm_g[i]), o_mla_c, gt_c,
                                   w_out_a[i], w_out_b[i], w_o[i])
            ctx = ctx + mod_c[2] * mix_c
            ctx = ctx + mod_c[5] * expert_choice_moe(modulate(ctx, norm2_g[i], mod_c[3], mod_c[4]),
                                                     router_w[i], w_gate[i], w_up[i], w_down[i])

        h2 = modulate(x_mid, norm2_g[i], mod_x[3], mod_x[4])
        x = x_mid + mod_x[5] * expert_choice_moe(h2, router_w[i], w_gate[i], w_up[i], w_down[i])
    return x


def setup_inputs(seed=0):
    out = dict(first_inputs(seed))
    for name, value in second_inputs(seed + 1).items():
        if name != "x":
            out[name + "_2"] = value
    return out


def reference(
    x, mem, mem_norm, l0_norm, l0_w_in, l0_a_vnorm, l0_a_ws, l0_a_bs, l0_b_qnorm, l0_b_knorm,
    l0_b_lq1, l0_b_lk1, l0_b_lq2, l0_b_lk2, l0_b_subln, l0_m_wkv, l0_m_qnorm, l0_m_knorm,
    l0_w_out, l1_norm, l1_w_in, l1_c_conv_w, l1_c_conv_b, l1_c_norm, l1_d_qnorm, l1_d_knorm,
    l1_d_cmp_pos_k, l1_d_cmp_w1_k, l1_d_cmp_w2_k, l1_d_cmp_pos_v, l1_d_cmp_w1_v, l1_d_cmp_w2_v,
    l1_m_wkv, l1_m_qnorm, l1_m_knorm, l1_w_out, c_2, ctx_2, c_ctx_2, ada_w_2, ada_b_2,
    norm1_g_2, norm2_g_2, w_in_2, conv_w_2, a_log_2, dt_bias_2, dn_norm_g_2, w_out_a_2,
    q_a_norm_g_2, w_uq_2, kv_a_norm_g_2, w_ukv_2, q_norm_g_2, k_norm_g_2, w_out_b_2, w_o_2,
    router_w_2, w_gate_2, w_up_2, w_down_2,
):
    x = first_block(
        x, mem, mem_norm, l0_norm, l0_w_in, l0_a_vnorm, l0_a_ws, l0_a_bs, l0_b_qnorm,
        l0_b_knorm, l0_b_lq1, l0_b_lk1, l0_b_lq2, l0_b_lk2, l0_b_subln, l0_m_wkv, l0_m_qnorm,
        l0_m_knorm, l0_w_out, l1_norm, l1_w_in, l1_c_conv_w, l1_c_conv_b, l1_c_norm, l1_d_qnorm,
        l1_d_knorm, l1_d_cmp_pos_k, l1_d_cmp_w1_k, l1_d_cmp_w2_k, l1_d_cmp_pos_v, l1_d_cmp_w1_v,
        l1_d_cmp_w2_v, l1_m_wkv, l1_m_qnorm, l1_m_knorm, l1_w_out,
    )
    return second_block(
        x, c_2, ctx_2, c_ctx_2, ada_w_2, ada_b_2, norm1_g_2, norm2_g_2, w_in_2, conv_w_2,
        a_log_2, dt_bias_2, dn_norm_g_2, w_out_a_2, q_a_norm_g_2, w_uq_2, kv_a_norm_g_2,
        w_ukv_2, q_norm_g_2, k_norm_g_2, w_out_b_2, w_o_2, router_w_2, w_gate_2, w_up_2,
        w_down_2,
    )


_drawn_inputs = setup_inputs


def setup_inputs(seed=0):
    import zlib

    import numpy as np

    out = dict(_drawn_inputs(seed))
    spreads = {}
    factors = {'mem_norm': 8.0,
     'l0_a_vnorm': 5.561,
     'l0_b_qnorm': 2.946,
     'l0_b_knorm': 2.867,
     'l0_b_lk1': 3.547,
     'l0_b_lq2': 8.0,
     'l0_b_subln': 3.591,
     'l0_m_qnorm': 8.0,
     'l0_m_knorm': 8.0,
     'l1_c_conv_b': 4.697,
     'l1_c_norm': 3.549,
     'l1_d_qnorm': 8.0,
     'l1_d_knorm': 8.0,
     'l1_d_cmp_pos_k': 8.0,
     'l1_d_cmp_pos_v': 8.0,
     'l1_m_qnorm': 8.0,
     'l1_m_knorm': 8.0,
     'ctx_2': 2.706,
     'ada_b_2': 2.668,
     'norm1_g_2': 5.609,
     'norm2_g_2': 3.759,
     'dn_norm_g_2': 7.281,
     'q_a_norm_g_2': 8.0,
     'kv_a_norm_g_2': 8.0,
     'q_norm_g_2': 8.0,
     'k_norm_g_2': 8.0}
    for name, (base, spread) in spreads.items():
        noise = np.random.default_rng([zlib.crc32(name.encode()), seed]).standard_normal(out[name].shape)
        drawn = base * np.exp(spread * noise) if base else spread * noise
        out[name] = jnp.asarray(drawn.astype(out[name].dtype))
    for name, factor in factors.items():
        out[name] = (out[name] * factor).astype(out[name].dtype)
    return out
```

```python
from contextlib import ExitStack
import math

import numpy as np

import concourse.bass as bass
from concourse import mybir

F32 = mybir.dt.float32
ALU = mybir.AluOpType
ACT = mybir.ActivationFunctionType
AX_X = mybir.AxisListType.X

P = 128
D = 1024
KD = D // P
SEQ = 512
TX = SEQ // P
MEM = 256
TM = MEM // P
EPS = 1e-6
SLOT = 4096
SLOTS = 3
NEG = -1e30
TINY = float(np.finfo(np.float32).tiny)
LAM_INIT = 0.8 - 0.6 * math.exp(-0.3 * 1)


class Counter:

    def __init__(self, sem, base):
        self.sem = sem
        self.base = base

    def __call__(self, n):
        return self.base + n


class Steps:

    def __init__(self, sem):
        self.sem = sem
        self.count = 0

    def __call__(self, eng, ins):
        self.count += 1
        ins.then_inc(self.sem, 1)
        eng.wait_ge(self.sem, self.count)


class Kit:

    def __init__(self, nc, stack):
        self.nc = nc
        self.stack = stack
        self.sems = {}
        self.totals = {}
        self.ps = stack.enter_context(nc.psum_tensor("banks", [P, 8, 512], F32))
        self.dve_step = Steps(self.sem("dve_step"))
        self.act_step = Steps(self.sem("act_step"))
        self.pool_step = Steps(self.sem("pool_step"))
        self.n_names = 0
        self.place = {}

    def sem(self, name):
        if name not in self.sems:
            self.sems[name] = self.stack.enter_context(self.nc.semaphore(name))
            self.totals[name] = 0
        return self.sems[name]

    def counter(self, name, total):
        sem = self.sem(name)
        base = self.totals[name]
        self.totals[name] += total
        return Counter(sem, base)

    def place_constants(self, stack, name, place):
        width = max(at + n for at, n in place.values())
        const = self.sb(stack, name, [P, width])
        self.place |= {k: (const, at, n) for k, (at, n) in place.items()}
        return const

    def part(self, name, tiles=1):
        const, at, n = self.place[name]
        c = const[:, at:at + n]
        return c if tiles == 1 else c.rearrange("p (t n) -> p t n", t=tiles)

    def sb(self, stack, name, shape):
        self.n_names += 1
        return stack.enter_context(self.nc.sbuf_tensor(f"{name}_{self.n_names}", shape, F32))


class WeightStream:

    def __init__(self, kit, stack):
        self.ring = kit.sb(stack, "weight_ring", [P, SLOTS, SLOT])
        self.landed = [kit.sem(f"weights_landed_{s}") for s in range(SLOTS)]
        self.used = kit.sem("weights_used")
        self.plan = []
        self.goal = []
        self.issued = 0

    def _plan(self, nk, nn, parts):
        i = len(self.plan)
        before = self.goal[i - SLOTS] if i >= SLOTS else 0
        self.plan.append((nk, nn, parts))
        self.goal.append(before + 16 * len(parts))
        return i

    def add(self, src, nk, nn):
        return self._plan(nk, nn, [(0, P, src.rearrange("(k p) n -> p k n", p=P))])

    def add_twice(self, src):
        nk = src.shape[0] // 64
        s = src.rearrange("(k p) n -> p k n", p=64)
        return self._plan(nk, src.shape[1], [(0, 64, s), (64, P, s)])

    def chunk(self, i):
        nk, nn, _ = self.plan[i]
        return self.ring[:, i % SLOTS, 0:nk * nn].rearrange("p (k n) -> p k n", k=nk)

    def load_ahead(self, sp, done, ahead=SLOTS):
        while self.issued < min(done + ahead, len(self.plan)):
            i = self.issued
            if i >= SLOTS:
                sp.wait_ge(self.used, i - SLOTS + 1)
            for p0, p1, src in self.plan[i][2]:
                sp.dma_start(self.chunk(i)[p0:p1], src).then_inc(self.landed[i % SLOTS], 16)
            self.issued += 1

    def arrived(self, pe, i):
        pe.wait_ge(self.landed[i % SLOTS], self.goal[i])


class Matrix:

    def __init__(self, stream, w, col_groups, k_step):
        rows = w.shape[0]
        nk = rows // P
        self.nk = nk
        self.groups = []
        for n0, nn in col_groups:
            chunks = []
            for k0 in range(0, nk, k_step):
                kk = min(k_step, nk - k0)
                chunks.append((stream.add(w[k0 * P:(k0 + kk) * P, n0:n0 + nn], kk, nn), k0, kk))
            self.groups.append((n0, nn, chunks))
        self.last = self.groups[-1][2][-1][0]


def columns(n0, n1, step=512):
    return [(a, min(step, n1 - a)) for a in range(n0, n1, step)]


def project(kit, stream, matrix, units, engines=2, ahead=SLOTS):
    nc = kit.nc
    work = []
    for n0, nn, chunks in matrix.groups:
        work.append((chunks, units(n0, nn)))
    total = sum(len(us) for _, us in work)
    products = kit.counter("products", total)
    taken = [kit.counter("taken_dve", len(range(0, total, engines))), kit.counter("taken_act", len(range(1, total, 2)) if engines == 2 else 0)]
    flat = [u for _, us in work for u in us]

    with nc.Block() as block:

        @block.sync
        def _(sp):
            stream.load_ahead(sp, matrix.last + 1, ahead)

        @block.tensor
        def _(pe):
            first = 0
            for chunks, us in work:
                for c, (i, k0, kk) in enumerate(chunks):
                    stream.arrived(pe, i)
                    w = stream.chunk(i)
                    for n, (m, cols, operands, _) in enumerate(us):
                        u = first + n
                        if c == 0 and u >= 8:
                            pe.wait_ge(taken[u % engines].sem, taken[u % engines]((u - 8) // engines + 1))
                        for j in range(kk):
                            lhsT, rhs = operands(w, j, k0 + j)
                            ins = nc.tensor.matmul(kit.ps[0:m, u % 8, 0:cols], lhsT, rhs,
                                                   start=(k0 + j == 0), stop=(k0 + j == matrix.nk - 1))
                        if c == len(chunks) - 1 and n < len(us) - 1:
                            ins.then_inc(products.sem, 1)
                    if c == len(chunks) - 1:
                        ins.then_inc(products.sem, 1)
                        pe.wait_ge(products.sem, products(first + len(us)))
                        pe.sem_inc(stream.used, 1)
                    else:
                        ins.then_inc(stream.used, 1)
                first += len(us)

        @block.vector
        def _(dve):
            for u in range(0, total, engines):
                m, cols, _, put = flat[u]
                dve.wait_ge(products.sem, products(u + 1))
                put(dve, False, kit.ps[0:m, u % 8, 0:cols]).then_inc(taken[0].sem, 1)

        @block.scalar
        def _(act):
            for u in (range(1, total, 2) if engines == 2 else ()):
                m, cols, _, put = flat[u]
                act.wait_ge(products.sem, products(u + 1))
                put(act, True, kit.ps[0:m, u % 8, 0:cols]).then_inc(taken[1].sem, 1)


def put_copy(kit, dst):
    def put(eng, act, psum):
        if act:
            return kit.nc.scalar.activation(dst, psum, ACT.Copy)
        return kit.nc.vector.tensor_copy(dst, psum)
    return put


def by_tokens(kit, turned, tiles, dst):
    def units(n0, nn):
        def unit(t):
            def operands(w, j, k):
                return turned[:, k, t * P:(t + 1) * P], w[:, j, :]
            return P, nn, operands, put_copy(kit, dst(t, n0, nn))
        return [unit(t) for t in tiles]
    return units


def norm_and_turn(kit, src, tiles, dst, gain, shift=None):
    nc = kit.nc
    T = len(tiles)
    nk = src.shape[2] // P
    ng = nk // 4
    with ExitStack() as st:
        sq = kit.sb(st, "squares", [P, src.shape[2]])
        ss = kit.sb(st, "square_sums", [P, T])
        xs = kit.sb(st, "scaled_rows", [P, 2, src.shape[2]])
        sums = kit.counter("row_sums", T)
        rooted = kit.counter("roots_ready", 1)
        scaled = kit.counter("rows_scaled", T)
        turned = kit.counter("turned", T * ng)
        taken = [kit.counter("taken_dve", T * (ng // 2)), kit.counter("taken_act", T * (ng // 2))]
        assert ng == 2

        def take(eng, act, i):
            g = 2 * i + (1 if act else 0)
            eng.wait_ge(turned.sem, turned(g + 1))
            for q in range(4):
                k = 4 * (g % 2) + q
                t = tiles[i]
                ps = kit.ps[:, g % 8, q * P:(q + 1) * P]
                out = dst[:, k, t * P:(t + 1) * P]
                if act:
                    ins = nc.scalar.activation(out, ps, ACT.Identity, scale=gain[:, k:k + 1],
                                               bias=0.0 if shift is None else shift[:, k:k + 1])
                elif shift is None:
                    ins = nc.vector.tensor_scalar(out, ps, gain[:, k:k + 1], None, ALU.mult)
                else:
                    ins = nc.vector.tensor_scalar(out, ps, gain[:, k:k + 1], shift[:, k:k + 1], ALU.mult, ALU.add)
            ins.then_inc(taken[g % 2].sem, 1)

        with nc.Block() as block:

            @block.scalar
            def _(act):
                for i, t in enumerate(tiles):
                    if i >= 1:
                        act.wait_ge(sums.sem, sums(i))
                    nc.scalar.activation(sq[:, :], src[:, t, :], ACT.Square, scale=src.shape[2] ** -0.5, accum_out=ss[:, i:i + 1]).then_inc(sums.sem, 1)
                act.wait_ge(sums.sem, sums(T))
                root(kit, ss[:, 0:T]).then_inc(rooted.sem, 1)
                for i in range(T):
                    take(act, True, i)

            @block.vector
            def _(dve):
                def scale(i):
                    if i >= 2:
                        dve.wait_ge(turned.sem, turned(ng * (i - 1)))
                    nc.vector.tensor_scalar(xs[:, i % 2, :], src[:, tiles[i], :], ss[:, i:i + 1], None, ALU.mult).then_inc(scaled.sem, 1)
                dve.wait_ge(rooted.sem, rooted(1))
                kit.dve_step(dve, nc.vector.reciprocal(ss[:, :], ss[:, :]))
                scale(0)
                for i in range(T):
                    if i + 1 < T:
                        scale(i + 1)
                    take(dve, False, i)

            @block.tensor
            def _(pe):
                for i in range(T):
                    pe.wait_ge(scaled.sem, scaled(i + 1))
                    for h in range(ng):
                        g = ng * i + h
                        if g >= 8:
                            pe.wait_ge(taken[g % 2].sem, taken[g % 2]((g - 8) // 2 + 1))
                        for q in range(4):
                            k = 4 * h + q
                            ins = nc.tensor.transpose(kit.ps[:, g % 8, q * P:(q + 1) * P], xs[:, i % 2, k * P:(k + 1) * P], kit.ident[:, :])
                        ins.then_inc(turned.sem, 1)


def turn(kit, groups):
    nc = kit.nc
    G = len(groups)
    turned = kit.counter("turned", G)
    taken = [kit.counter("taken_dve", (G + 1) // 2), kit.counter("taken_act", G // 2)]

    def bank(g):
        srcs, dst = groups[g]
        p, w = srcs[0].shape
        return kit.ps[0:w, g % 8, 0:len(srcs) * p].rearrange("w (n p) -> w n p", p=p)

    with nc.Block() as block:

        @block.tensor
        def _(pe):
            for g, (srcs, _) in enumerate(groups):
                if g >= 8:
                    pe.wait_ge(taken[g % 2].sem, taken[g % 2]((g - 8) // 2 + 1))
                for n, s in enumerate(srcs):
                    ins = nc.tensor.transpose(bank(g)[:, n, :], s, kit.ident[0:s.shape[0], 0:s.shape[0]])
                ins.then_inc(turned.sem, 1)

        @block.vector
        def _(dve):
            for g in range(0, G, 2):
                dve.wait_ge(turned.sem, turned(g + 1))
                nc.vector.tensor_copy(groups[g][1], bank(g)).then_inc(taken[0].sem, 1)

        @block.scalar
        def _(act):
            for g in range(1, G, 2):
                act.wait_ge(turned.sem, turned(g + 1))
                nc.scalar.activation(groups[g][1], bank(g), ACT.Copy).then_inc(taken[1].sem, 1)


def attend(kit, units, scale):
    nc = kit.nc
    U = len(units)
    with ExitStack() as st:
        probs = kit.sb(st, "probs", [P, 2, 1024])
        probs_turned = kit.sb(st, "probs_turned", [P, 2, 768])
        shift = kit.sb(st, "minus_max", [P, 4, 2])
        sums = kit.sb(st, "prob_sums", [P, 4, 2])
        inv = kit.sb(st, "inverse_sums", [P, 4, 2])
        scored = kit.counter("scored", U)
        max_ready = kit.counter("max_ready", U)
        exp_ready = kit.counter("exp_ready", U)
        weighed = [u for u in range(U) if len(units[u]["maps"]) == 2 or units[u].get("mask")]
        probs_ready = kit.counter("probs_ready", len(weighed))
        turned = kit.counter("probs_turned", U)
        kept = [kit.counter("turned_kept_dve", (U + 1) // 2), kit.counter("turned_kept_act", U // 2)]
        summed = kit.counter("values_summed", U)
        finished = kit.counter("finished", U)

        def maps_of(u):
            return len(units[u]["maps"])

        def score_banks(u):
            x = units[u]
            b = 2 * (u % 2)
            if maps_of(u) == 2:
                return kit.ps[:, b:b + 2, 0:x["n"]]
            return kit.ps[:, b:b + 2, :].rearrange("p b n -> p (b n)")[:, 0:x["n"]].unsqueeze(1)

        def probs_of(u):
            x = units[u]
            if maps_of(u) == 2:
                return probs[:, u % 2, :].rearrange("p (m n) -> p m n", m=2)[:, :, 0:x["n"]]
            return probs[:, u % 2, 0:x["n"]].unsqueeze(1)

        def blocks(u):
            n = units[u]["n"]
            return [(a, min(P, n - a)) for a in range(0, n, P)]

        def turned_bank(u):
            nb, w = len(blocks(u)), blocks(u)[0][1]
            if nb <= 4:
                return kit.ps[0:w, 4 + u % 2, 0:nb * P]
            return kit.ps[:, 4:6, :].rearrange("p b n -> p (b n)")[:, 0:nb * P]

        with nc.Block() as block:

            @block.tensor
            def _(pe):
                def scores(u):
                    x = units[u]
                    if u >= 2:
                        pe.wait_ge(exp_ready.sem, exp_ready(u - 1))
                    for m, (q, k) in enumerate(x["maps"]):
                        for a in range(0, x["n"], 512):
                            b = min(a + 512, x["n"])
                            bank = 2 * (u % 2) + m + a // 512
                            more = x.get("more")
                            ins = nc.tensor.matmul(kit.ps[:, bank, 0:b - a], q, k[:, a:b], start=True, stop=not more)
                            if more:
                                ins = nc.tensor.matmul(kit.ps[:, bank, 0:b - a], more[0], more[1][:, a:b], start=False, stop=True)
                    ins.then_inc(scored.sem, 1)

                def turn_probs(u):
                    if u in weighed:
                        pe.wait_ge(probs_ready.sem, probs_ready(weighed.index(u) + 1))
                    pe.wait_ge(exp_ready.sem, exp_ready(u + 1))
                    v = u - 2 if len(blocks(u)) <= 4 else u - 1
                    if v >= 0:
                        pe.wait_ge(kept[v % 2].sem, kept[v % 2](v // 2 + 1))
                    for b, (a, w) in enumerate(blocks(u)):
                        bank, at = (4 + u % 2, b) if len(blocks(u)) <= 4 else (4 + b // 4, b % 4)
                        ins = nc.tensor.transpose(kit.ps[0:w, bank, at * P:(at + 1) * P], probs[:, u % 2, a:a + w], kit.ident[:, :])
                    ins.then_inc(turned.sem, 1)

                def sum_values(u):
                    x = units[u]
                    pe.wait_ge(kept[u % 2].sem, kept[u % 2](u // 2 + 1))
                    if u >= 2:
                        pe.wait_ge(finished.sem, finished(u - 1))
                    for b, (a, w) in enumerate(blocks(u)):
                        v = x["values"][b]
                        ins = nc.tensor.matmul(kit.ps[:, 6 + u % 2, 0:v.shape[1]], probs_turned[0:w, u % 2, b * P:(b + 1) * P], v,
                                               start=(b == 0), stop=(b == len(blocks(u)) - 1))
                    ins.then_inc(summed.sem, 1)

                scores(0)
                for i in range(U + 2):
                    if i + 1 < U:
                        scores(i + 1)
                    if 1 <= i <= U:
                        turn_probs(i - 1)
                    if i >= 2:
                        sum_values(i - 2)

            def keep_turned(eng, act, u):
                eng.wait_ge(turned.sem, turned(u + 1))
                if u >= 2:
                    eng.wait_ge(summed.sem, summed(u - 1))
                src = turned_bank(u)
                dst = probs_turned[0:src.shape[0], u % 2, 0:src.shape[1]]
                if act:
                    nc.scalar.activation(dst, src, ACT.Copy).then_inc(kept[1].sem, 1)
                else:
                    nc.vector.tensor_copy(dst, src).then_inc(kept[0].sem, 1)

            @block.vector
            def _(dve):
                step = kit.dve_step

                def row_max(u):
                    x = units[u]
                    dve.wait_ge(scored.sem, scored(u + 1))
                    s = score_banks(u)
                    M = maps_of(u)
                    if x.get("causal"):
                        own = s[:, :, x["n"] - P:x["n"]]
                        step(dve, nc.vector.tensor_tensor(own, own, kit.causal[:, :].unsqueeze(1).broadcast_to([P, M, P]), ALU.add))
                    if x.get("mask"):
                        step(dve, nc.vector.tensor_tensor(s[:, 0, :], s[:, 0, :], x["mask"][0], ALU.add))
                    step(dve, nc.vector.tensor_reduce(shift[:, u % 4, 0:M], s, AX_X, ALU.max))
                    nc.vector.tensor_scalar(shift[:, u % 4, 0:M], shift[:, u % 4, 0:M], -scale, None, ALU.mult).then_inc(max_ready.sem, 1)

                def weigh(u):
                    x = units[u]
                    dve.wait_ge(exp_ready.sem, exp_ready(u + 1))
                    p = probs_of(u)
                    M = maps_of(u)
                    if x.get("mask"):
                        step(dve, nc.vector.tensor_tensor(p[:, 0, :], p[:, 0, :], x["mask"][1], ALU.mult))
                        step(dve, nc.vector.tensor_reduce(sums[:, u % 4, 0:1], p[:, 0, :], AX_X, ALU.add))
                        step(dve, nc.vector.tensor_scalar(sums[:, u % 4, 0:1], sums[:, u % 4, 0:1], TINY, None, ALU.max))
                    step(dve, nc.vector.reciprocal(inv[:, u % 4, 0:M], sums[:, u % 4, 0:M]))
                    if M == 2:
                        step(dve, nc.vector.tensor_scalar(inv[:, u % 4, 1:2], inv[:, u % 4, 1:2], kit.minus_lam[:, 0:1], None, ALU.mult))
                        step(dve, nc.vector.tensor_scalar(p[:, 0, :], p[:, 0, :], inv[:, u % 4, 0:1], None, ALU.mult))
                        step(dve, nc.vector.scalar_tensor_tensor(p[:, 0, :], p[:, 1, :], inv[:, u % 4, 1:2], p[:, 0, :], ALU.mult, ALU.add))
                    if u in weighed:
                        dve.sem_inc(probs_ready.sem, 1)

                def finish(u):
                    dve.wait_ge(summed.sem, summed(u + 1))
                    dv = units[u]["values"][0].shape[1]
                    units[u]["finish"](dve, kit.ps[:, 6 + u % 2, 0:dv], inv[:, u % 4, 0:1]).then_inc(finished.sem, 1)

                for i in range(U + 3):
                    if i < U:
                        row_max(i)
                    if 1 <= i <= U:
                        weigh(i - 1)
                    if 2 <= i <= U + 1 and i % 2 == 0:
                        keep_turned(dve, False, i - 2)
                    if i >= 3:
                        finish(i - 3)

            @block.scalar
            def _(act):
                for i in range(U + 2):
                    if i < U:
                        act.wait_ge(max_ready.sem, max_ready(i + 1))
                        if i >= 2:
                            act.wait_ge(turned.sem, turned(i - 1))
                        for m in range(maps_of(i)):
                            ins = nc.scalar.activation(probs_of(i)[:, m, :], score_banks(i)[:, m, :], ACT.Exp, scale=scale,
                                                       bias=shift[:, i % 4, m:m + 1], accum_out=sums[:, i % 4, m:m + 1])
                        ins.then_inc(exp_ready.sem, 1)
                    if i >= 2 and i % 2 == 1:
                        keep_turned(act, True, i - 2)


def mean_squares(kit, dve, sq, ms, parts):
    nc = kit.nc
    at = 0
    for src, _, _ in parts:
        n, G, d = src.shape
        s = sq[0:n, 0:G * d].rearrange("p (g n) -> p g n", g=G)
        kit.dve_step(dve, nc.vector.scalar_tensor_tensor(s, src, 1.0 / d, src, ALU.mult, ALU.mult))
        kit.dve_step(dve, nc.vector.tensor_reduce(ms[0:n, at:at + G], s, AX_X, ALU.add))
        at += G


def root(kit, ms):
    return kit.nc.scalar.activation(ms, ms, ACT.Sqrt, bias=kit.eps[0:ms.shape[0], :])


def scale_rows(kit, dve, ms, parts):
    nc = kit.nc
    n, G = parts[0][0].shape[0], sum(src.shape[1] for src, _, _ in parts)
    kit.dve_step(dve, nc.vector.reciprocal(ms[0:n, 0:G], ms[0:n, 0:G]))
    at = 0
    for src, dst, _ in parts:
        n, G, d = src.shape
        ins = nc.vector.tensor_tensor(dst, src, ms[0:n, at:at + G].unsqueeze(2).broadcast_to([n, G, d]), ALU.mult)
        at += G
    kit.dve_step(dve, ins)
    for src, dst, gain in parts:
        n, G, d = src.shape
        g = gain if len(gain.shape) == 3 else gain.unsqueeze(1).broadcast_to([n, G, d])
        ins = nc.vector.tensor_tensor(dst, dst, g, ALU.mult)
    kit.dve_step(dve, ins)


def rope(kit, dve, tmp, x1, x2, cos, sin):
    nc = kit.nc
    step = kit.dve_step
    n, H, half = x1.shape
    c = cos.unsqueeze(1).broadcast_to([n, H, half])
    s = sin.unsqueeze(1).broadcast_to([n, H, half])
    a, b, e, f = (tmp[0:n, i * H * half:(i + 1) * H * half].rearrange("p (h d) -> p h d", h=H) for i in range(4))
    nc.vector.tensor_tensor(a, x1, c, ALU.mult)
    nc.vector.tensor_tensor(b, x2, s, ALU.mult)
    nc.vector.tensor_tensor(e, x1, s, ALU.mult)
    step(dve, nc.vector.tensor_tensor(f, x2, c, ALU.mult))
    nc.vector.tensor_tensor(x1, a, b, ALU.subtract)
    step(dve, nc.vector.tensor_tensor(x2, e, f, ALU.add))



def rotation(pos, half, theta):
    inv = np.float32(theta) ** (-np.arange(half, dtype=np.float32) / np.float32(half))
    ang = np.asarray(pos, np.float32)[:, None] * inv[None, :].astype(np.float32)
    return np.cos(ang).astype(np.float32), np.sin(ang).astype(np.float32)


N_CMP = 31
CMP_STRIDE = 16
CMP_BLOCK = 32
GRID_W = 64
CHUNK = 64
N_EXPERTS = 16
CAP = 64


def tiled(a):
    return a.reshape(TX, P, -1).transpose(1, 0, 2).reshape(P, -1)


def constant_parts():
    i = np.arange(P)
    row, col = i[:, None], i[None, :]
    pos = np.arange(SEQ)
    parts = {"eps": np.full((P, 1), EPS), "ident": np.eye(P), "causal": np.where(col <= row, 0.0, NEG), "upper": (row <= col) * 1.0,
             "ones": np.ones((P, P))}
    for name, half in (("r4", 4), ("r8", 8)):
        c, s = rotation(pos, half, 500000.0)
        parts[name + "c"], parts[name + "s"] = tiled(c), tiled(s)
    ends = np.arange(N_CMP) * CMP_STRIDE + CMP_BLOCK - 1
    c, s = rotation(ends, 8, 500000.0)
    for name, a in (("endc", c), ("ends", s)):
        parts[name] = np.zeros((P, 8))
        parts[name][0:N_CMP] = a
    seen = ends[None, :] <= pos[:, None]
    parts["cmp_add"] = tiled(np.where(seen, 0.0, NEG))
    parts["cmp_mul"] = tiled(seen * 1.0)
    return spread(parts)


def spread(parts):
    return {k: np.broadcast_to(np.asarray(v, np.float32), (P, np.asarray(v).shape[1])) for k, v in parts.items()}


def second_constant_parts():
    i = np.arange(P)
    row, col = i[:, None], i[None, :]
    same = (row // CHUNK) == (col // CHUNK)
    parts = {}
    for d, before in (("f", col < row), ("b", col > row)):
        incl = same & (before | (row == col))
        parts["tri_" + d] = (incl.T) * 1.0
        parts["decay_t_" + d] = np.where(incl.T, 0.0, -NEG)
    parts["same"] = same * 1.0
    parts["half0"] = (row < CHUNK) * np.ones((1, P))
    parts["half1"] = (row >= CHUNK) * np.ones((1, P))
    s = 1
    while s < CHUNK:
        pair = (row // (2 * s)) == (col // (2 * s))
        parts[f"level_f{s}"] = (pair & (row % (2 * s) >= s) & (col % (2 * s) < s)) * 1.0
        parts[f"level_b{s}"] = parts[f"level_f{s}"].T
        s *= 2
    return spread(parts)


def third_constant_parts():
    pos = np.arange(SEQ)
    parts = {"slot_iota": np.arange(CAP)[None, :] + 1.0}
    for name, p in (("row", pos // GRID_W), ("col", pos % GRID_W)):
        c, s = rotation(p, 16, 10000.0)
        parts[name + "c"], parts[name + "s"] = tiled(c), tiled(s)
    return spread(parts)


def constants(parts):
    at, place = 0, {}
    for k, v in parts.items():
        place[k] = (at, v.shape[1])
        at += v.shape[1]
    return np.ascontiguousarray(np.concatenate(list(parts.values()), axis=1)), place


def load(kit, pairs):
    nc = kit.nc
    landed = kit.counter("loaded", 16 * len(pairs))
    with nc.Block() as block:

        @block.sync
        def _(sp):
            with nc.allow_non_contiguous_dma("columns of small vectors"):
                for dst, src in pairs:
                    sp.dma_start(dst, src).then_inc(landed.sem, 16)
            sp.wait_ge(landed.sem, landed(16 * len(pairs)))


def row_bc(v, n=P):
    return v.partition_broadcast(n)


def as_columns(v):
    return v.rearrange("(k p) -> p k", p=P)


def memory_attention_units(kit, mq_turned, mk_turned, mem_v, out):
    units = []
    for h in range(4):
        b = 64 * (h % 2)
        for t in range(TX):
            def finish(dve, psum, inv, h=h, t=t):
                return kit.nc.vector.tensor_scalar(out[:, t, h * 64:(h + 1) * 64], psum, inv, None, ALU.mult)
            units.append(dict(maps=[(mq_turned[b:b + 64, h // 2, t * P:(t + 1) * P], mk_turned[b:b + 64, h // 2, :])], n=MEM,
                              values=[mem_v[:, m, 256 + h * 64:256 + (h + 1) * 64] for m in range(TM)], finish=finish))
    return units


def load_matrices_first(stream, a):
    m = {}
    m["mem0"] = Matrix(stream, a["l0_m_wkv"], columns(0, 512), KD)
    m["in0"] = Matrix(stream, a["l0_w_in"], columns(0, 4096), KD)
    m["out0"] = Matrix(stream, a["l0_w_out"], columns(0, D), 5)
    m["mem1"] = Matrix(stream, a["l1_m_wkv"], columns(0, 512), KD)
    m["in1"] = Matrix(stream, a["l1_w_in"], columns(0, 2048) + [(2048, 256)] + columns(2304, 3864), KD)
    m["cmp_k"] = stream.add_twice(a["l1_d_cmp_w1_k"])
    m["cmp_v"] = stream.add_twice(a["l1_d_cmp_w1_v"])
    m["out1"] = Matrix(stream, a["l1_w_out"], columns(0, D), 5)
    return m


def elementwise(kit, vector=None, scalar=None, gpsimd=None, tensor=None, sync=None):
    with kit.nc.Block() as block:
        if vector:
            block.vector(vector)
        if scalar:
            block.scalar(scalar)
        if gpsimd:
            block.gpsimd(gpsimd)
        if tensor:
            block.tensor(tensor)
        if sync:
            block.sync(sync)


def residual_units(kit, x, turned):
    def units(n0, nn):
        def unit(t):
            def operands(w, j, k):
                return turned[:, k, t * P:(t + 1) * P], w[:, j, :]

            def put(eng, act, psum):
                dst = x[:, t, n0:n0 + nn]
                return kit.nc.vector.tensor_tensor(dst, dst, psum, ALU.add)
            return P, nn, operands, put
        return [unit(t) for t in range(TX)]
    return units


def turn_mix(kit, mix, turned):
    groups = []
    for k in range(mix.shape[2] // P):
        groups.append(([mix[:, t, k * P:(k + 1) * P] for t in range(TX)], turned[:, k, :].rearrange("p (t n) -> p t n", t=TX)))
    turn(kit, groups)


def first_layer(kit, stream, m, a, x, memT):
    nc = kit.nc
    step = kit.dve_step
    with ExitStack() as st:
        sb = lambda name, shape: kit.sb(st, name, shape)
        y = sb("projected", [P, TX, 4096])
        mem_kv = sb("memory_kv", [P, TM, 512])
        g_in = sb("gain_in", [P, KD])
        vn = sb("v_gain", [P, 512])
        qk_gain = sb("qk_gain", [P, 2, 32])
        sub = sb("sub_gain", [P, 64])
        mqk = sb("mqk_gain", [P, 2, 64])
        lq = sb("lambda_vectors", [P, 4, 32])
        lam = sb("lambda", [P, 4])
        ws = sb("spatial", [P, 4, P])
        bs = sb("spatial_bias", [4, P])
        load(kit, [(g_in[:, :], as_columns(a["l0_norm"])), (vn[:, :], row_bc(a["l0_a_vnorm"])),
                   (qk_gain[:, 0, :], row_bc(a["l0_b_qnorm"])), (qk_gain[:, 1, :], row_bc(a["l0_b_knorm"])),
                   (sub[:, :], row_bc(a["l0_b_subln"])), (mqk[:, 0, :], row_bc(a["l0_m_qnorm"])),
                   (mqk[:, 1, :], row_bc(a["l0_m_knorm"])),
                   (lq[:, 0, :], row_bc(a["l0_b_lq1"])), (lq[:, 1, :], row_bc(a["l0_b_lq2"])),
                   (lq[:, 2, :], row_bc(a["l0_b_lk1"])), (lq[:, 3, :], row_bc(a["l0_b_lk2"])),
                   (ws[:, :, :], a["l0_a_ws"].rearrange("g t s -> t g s")), (bs[:, :], a["l0_a_bs"])])
        with ExitStack() as hs:
            hT = kit.sb(hs, "rows_turned", [P, KD, SEQ])
            norm_and_turn(kit, x, list(range(TX)), hT, g_in)
            project(kit, stream, m["mem0"], by_tokens(kit, memT, range(TM), lambda t, n0, nn: mem_kv[:, t, n0:n0 + nn]))
            project(kit, stream, m["in0"], by_tokens(kit, hT, range(TX), lambda t, n0, nn: y[:, t, n0:n0 + nn]))

        U, V, AG, BQ, BK, BV, BG, MQ, MG = 0, 512, 1024, 1536, 2048, 2560, 3072, 3584, 3840
        vnorm = sb("v_normed", [P, TX, 512])
        ready = kit.counter("activated", TX)
        lam_ready = kit.counter("lambda_sums", 1)
        lam_exp = kit.counter("lambda_exps", 1)
        with ExitStack() as es:
            sq = kit.sb(es, "squares", [P, 1024])
            ms = kit.sb(es, "mean_squares", [P, TX * 36 + TM * 4 + TX * 4])
            sums = kit.counter("mean_squares_ready", 2)
            roots = kit.counter("roots_ready", 2)
            heads = lambda v, d: v.rearrange("p (h d) -> p h d", d=d)
            parts = []
            for t in range(TX):
                for n0, nn, d, gain in ((BQ, 512, 32, qk_gain[:, 0, :]), (BK, 512, 32, qk_gain[:, 1, :]), (MQ, 256, 64, mqk[:, 0, :])):
                    v = heads(y[:, t, n0:n0 + nn], d)
                    parts.append((v, v, gain))
            for t in range(TM):
                v = heads(mem_kv[:, t, 0:256], 64)
                parts.append((v, v, mqk[:, 1, :]))
            v_parts = [(heads(y[:, t, V:V + 512], P), heads(vnorm[:, t, :], P), heads(vn[:, :], P)) for t in range(TX)]
            n_first = TX * 36 + TM * 4

            def vector(dve):
                step(dve, nc.vector.tensor_tensor(lq[:, 0:2, :], lq[:, 0:2, :], lq[:, 2:4, :], ALU.mult))
                nc.vector.tensor_reduce(lam[:, 0:2], lq[:, 0:2, :], AX_X, ALU.add).then_inc(lam_ready.sem, 1)
                mean_squares(kit, dve, sq, ms[:, 0:n_first], parts)
                dve.sem_inc(sums.sem, 1)
                dve.wait_ge(roots.sem, roots(1))
                scale_rows(kit, dve, ms[:, 0:n_first], parts)
                for t in range(TX):
                    v = y[:, t, BQ:BQ + 1024].rearrange("p (h d) -> p h d", h=32)
                    rope(kit, dve, sq, v[:, :, 0:4], v[:, :, 4:8], kit.part("r4c", TX)[:, t, :], kit.part("r4s", TX)[:, t, :])
                dve.wait_ge(lam_exp.sem, lam_exp(1))
                step(dve, nc.vector.tensor_tensor(lam[:, 0:1], lam[:, 2:3], lam[:, 3:4], ALU.subtract))
                step(dve, nc.vector.tensor_scalar(kit.minus_lam[:, 0:1], lam[:, 0:1], LAM_INIT, -1.0, ALU.add, ALU.mult))
                dve.wait_ge(ready.sem, ready(TX))
                mean_squares(kit, dve, sq, ms[:, n_first:], v_parts)
                dve.sem_inc(sums.sem, 1)
                dve.wait_ge(roots.sem, roots(2))
                scale_rows(kit, dve, ms[:, n_first:], v_parts)

            def scalar(act):
                act.wait_ge(lam_ready.sem, lam_ready(1))
                nc.scalar.activation(lam[:, 2:4], lam[:, 0:2], ACT.Exp).then_inc(lam_exp.sem, 1)
                act.wait_ge(sums.sem, sums(1))
                root(kit, ms[:, 0:n_first]).then_inc(roots.sem, 1)
                for t in range(TX):
                    nc.scalar.activation(y[:, t, U:U + 1024], y[:, t, U:U + 1024], ACT.Gelu_apprx_tanh).then_inc(ready.sem, 1)
                act.wait_ge(sums.sem, sums(2))
                root(kit, ms[:, n_first:]).then_inc(roots.sem, 1)
                for n0, nn in ((AG, 512), (BG, 512), (MG, 256)):
                    kit.act_step(act, nc.scalar.activation(y[:, :, n0:n0 + nn], y[:, :, n0:n0 + nn], ACT.Silu))

            elementwise(kit, vector=vector, scalar=scalar)

        ts = ExitStack()
        qT = kit.sb(ts, "queries_turned", [P, 4, SEQ])
        kT = kit.sb(ts, "keys_turned", [P, 4, SEQ])
        mqT = kit.sb(ts, "mem_queries_turned", [P, 2, SEQ])
        mkT = kit.sb(ts, "mem_keys_turned", [P, 2, MEM])
        wsT = kit.sb(ts, "spatial_turned", [P, 4, P])
        bsT = kit.sb(ts, "spatial_bias_turned", [P, 4])
        groups = []
        for dst, n0, nf in ((qT, BQ, 4), (kT, BK, 4), (mqT, MQ, 2)):
            for f in range(nf):
                groups.append(([y[:, t, n0 + f * P:n0 + (f + 1) * P] for t in range(TX)], dst[:, f, :].rearrange("p (t n) -> p t n", t=TX)))
        for f in range(2):
            groups.append(([mem_kv[:, t, f * P:(f + 1) * P] for t in range(TM)], mkT[:, f, :].rearrange("p (t n) -> p t n", t=TM)))
        groups.append(([ws[:, g, :] for g in range(4)], wsT[:, :, :]))
        groups.append(([bs[:, :]], bsT[:, :].unsqueeze(1)))
        turn(kit, groups)

        masked = kit.counter("spatial_masked", 1)
        mixed = kit.counter("spatial_mixed", 4)

        def sgu_vector(dve):
            nc.vector.tensor_tensor(wsT[:, :, :], wsT[:, :, :], kit.part("upper").unsqueeze(1).broadcast_to([P, 4, P]), ALU.mult).then_inc(masked.sem, 1)
            for g in range(4):
                dve.wait_ge(mixed.sem, mixed(g + 1))
                u = y[:, :, U + g * P:U + (g + 1) * P]
                step(dve, nc.vector.scalar_tensor_tensor(u, kit.ps[:, g, :].rearrange("p (t d) -> p t d", t=TX), bsT[:, g:g + 1], u, ALU.add, ALU.mult))
                step(dve, nc.vector.tensor_tensor(u, u, y[:, :, AG + g * P:AG + (g + 1) * P], ALU.mult))

        def sgu_tensor(pe):
            pe.wait_ge(masked.sem, masked(1))
            for g in range(4):
                nc.tensor.matmul(kit.ps[:, g, :].rearrange("p (t d) -> p t d", t=TX), wsT[:, g, :], vnorm[:, :, g * P:(g + 1) * P],
                                 start=True, stop=True).then_inc(mixed.sem, 1)

        elementwise(kit, vector=sgu_vector, tensor=sgu_tensor)

        units = []
        for h in range(8):
            for t in range(TX):
                def finish(dve, psum, inv, h=h, t=t):
                    return nc.vector.tensor_copy(y[:, t, V + h * 64:V + (h + 1) * 64], psum)
                maps = []
                for mm in range(2):
                    c = 2 * h + mm
                    b = 32 * (c % 4)
                    maps.append((qT[b:b + 32, c // 4, t * P:(t + 1) * P], kT[b:b + 32, c // 4, 0:(t + 1) * P]))
                units.append(dict(maps=maps, n=(t + 1) * P, causal=True,
                                  values=[y[:, s, BV + h * 64:BV + (h + 1) * 64] for s in range(t + 1)], finish=finish))
        attend(kit, units, 32 ** -0.5)
        attend(kit, memory_attention_units(kit, mqT, mkT, mem_kv, y[:, :, AG:AG + 256]), 64 ** -0.5)
        ts.close()
        with ExitStack() as es:
            sq = kit.sb(es, "squares", [P, 1024])
            ms = kit.sb(es, "mean_squares", [P, TX * 8])
            sums = kit.counter("mean_squares_ready", 1)
            roots = kit.counter("roots_ready", 1)
            parts = []
            for t in range(TX):
                v = y[:, t, V:V + 512].rearrange("p (h d) -> p h d", h=8)
                parts.append((v, v, sub[:, :]))

            def gate_root(act):
                act.wait_ge(sums.sem, sums(1))
                root(kit, ms[:, :]).then_inc(roots.sem, 1)

            def gate_vector(dve):
                mean_squares(kit, dve, sq, ms, parts)
                dve.sem_inc(sums.sem, 1)
                step(dve, nc.vector.tensor_tensor(y[:, :, AG:AG + 256], y[:, :, AG:AG + 256], y[:, :, MG:MG + 256], ALU.mult))
                dve.wait_ge(roots.sem, roots(1))
                scale_rows(kit, dve, ms, parts)
                step(dve, nc.vector.scalar_tensor_tensor(y[:, :, V:V + 512], y[:, :, V:V + 512], 1.0 - LAM_INIT, y[:, :, BG:BG + 512], ALU.mult, ALU.mult))
            elementwise(kit, vector=gate_vector, scalar=gate_root)
        with ExitStack() as es:
            mixT = kit.sb(es, "mix_turned", [P, 10, SEQ])
            turn_mix(kit, y[:, :, 0:1280], mixT)
            project(kit, stream, m["out0"], residual_units(kit, x, mixT), engines=1)


def second_layer(kit, stream, m, a, x, memT):
    nc = kit.nc
    step = kit.dve_step
    with ExitStack() as st:
        sb = lambda name, shape: kit.sb(st, name, shape)
        PAD = 30
        tb = sb("projected", [P, TX, 2584])
        conv_a = sb("conv_input", [P, 4, PAD + SEQ])
        conv_y = sb("conv_output", [P, 4, SEQ])
        raw = sb("compress_input", [P, 2, SEQ])
        mem_kv = sb("memory_kv", [P, TM, 512])
        g_in = sb("gain_in", [P, KD])
        cw = sb("conv_w", [31, 512])
        cwT = sb("conv_w_turned", [P, 4, 31])
        cb = sb("conv_b", [P, 4])
        cn = sb("conv_gain", [P, 512])
        dqk = sb("qk_gain", [P, 2, 64])
        mqk = sb("mqk_gain", [P, 2, 64])
        posT = sb("pos_turned", [P, 2, CMP_BLOCK])
        w2 = sb("compress_w2", [P, 2, 64])
        pos_pairs = []
        for i, n in enumerate(("k", "v")):
            for g in range(2):
                pos_pairs.append((posT[64 * g:64 * g + 64, i, :], a[f"l1_d_cmp_pos_{n}"].rearrange("l h -> h l")))
            pos_pairs.append((w2[:, i, :], a[f"l1_d_cmp_w2_{n}"]))
        load(kit, [(g_in[:, :], as_columns(a["l1_norm"])), (cw[:, :], a["l1_c_conv_w"]), (cb[:, :], as_columns(a["l1_c_conv_b"])),
                   (cn[:, :], row_bc(a["l1_c_norm"])), (dqk[:, 0, :], row_bc(a["l1_d_qnorm"])), (dqk[:, 1, :], row_bc(a["l1_d_knorm"])),
                   (mqk[:, 0, :], row_bc(a["l1_m_qnorm"])), (mqk[:, 1, :], row_bc(a["l1_m_knorm"]))] + pos_pairs)
        CG, DQ, KV, BGT, DG, MQ, MG = 0, 512, 1024, 1536, 1560, 2072, 2328
        with ExitStack() as hs:
            hT = kit.sb(hs, "rows_turned", [P, KD, SEQ])
            norm_and_turn(kit, x, list(range(TX)), hT, g_in)
            project(kit, stream, m["mem1"], by_tokens(kit, memT, range(TM), lambda t, n0, nn: mem_kv[:, t, n0:n0 + nn]))

            def units(n0, nn):
                if n0 >= 2304 or 1024 <= n0 < 2048:
                    off = 1024 if n0 < 2048 else 1280
                    return by_tokens(kit, hT, range(TX), lambda t, n0, nn: tb[:, t, n0 - off:n0 - off + nn])(n0, nn)

                def unit(f):
                    def operands(w, j, k):
                        return w[:, j, f * P:(f + 1) * P], hT[:, k, :]
                    dst = conv_a[:, f, PAD:] if n0 == 0 else conv_y[:, f, :] if n0 == 512 else raw[:, f, :]
                    return P, SEQ, operands, put_copy(kit, dst)
                return [unit(f) for f in range(nn // P)]
            project(kit, stream, m["in1"], units)

        turn(kit, [([cw[:, f * P:(f + 1) * P] for f in range(4)], cwT[:, :, :])])

        kd = sb("keys_twice", [P, TX, 2, 2, 2, 64])
        kcd = sb("compressed_keys_twice", [32, 2, 2, 64])
        vc = sb("compressed_values", [32, 2, 64])
        hid = sb("compressed_hidden", [P, 2, 2 * N_CMP])
        conv_gate = kit.counter("conv_gate", 1)
        blocks_ready = kit.counter("blocks_ready", 2)
        hid_sum = kit.counter("hidden_sums", 2)
        hid_ready = kit.counter("hidden_ready", 2)
        kv_ready = kit.counter("compressed_ready", 2)
        with ExitStack() as es:
            blk = kit.sb(es, "blocks", [P, 2, CMP_BLOCK, N_CMP])
            sq = kit.sb(es, "squares", [P, 1024])
            ms = kit.sb(es, "mean_squares", [P, TX * 16 + TM * 4 + 2])
            n_first = TX * 16 + TM * 4
            sums = kit.counter("mean_squares_ready", 2)
            roots = kit.counter("roots_ready", 2)
            heads = lambda v: v.rearrange("p (h d) -> p h d", d=64)
            parts = []
            for t in range(TX):
                v = heads(tb[:, t, DQ:DQ + 512])
                parts.append((v, v, dqk[:, 0, :]))
                for kind in range(2):
                    parts.append((heads(tb[:, t, KV + 256 * kind:KV + 256 * kind + 128]), kd[:, t, kind, :, 0, :], dqk[:, 1, :]))
                v = heads(tb[:, t, MQ:MQ + 256])
                parts.append((v, v, mqk[:, 0, :]))
            for t in range(TM):
                v = heads(mem_kv[:, t, 0:256])
                parts.append((v, v, mqk[:, 1, :]))
            ck = kcd[0:N_CMP, :, 0, :]
            cmp_parts = [(ck, ck, dqk[0:N_CMP, 1, :])]

            def vector(dve):
                for i in range(2):
                    for r in range(2):
                        src = raw[:, i, 16 * r:16 * r + 16 * N_CMP].rearrange("p (b l) -> p l b", l=16)
                        ins = nc.vector.tensor_tensor(blk[:, i, 16 * r:16 * r + 16, :], src,
                                                      posT[:, i, 16 * r:16 * r + 16].unsqueeze(2).broadcast_to([P, 16, N_CMP]), ALU.add)
                    ins.then_inc(blocks_ready.sem, 1)
                step(dve, nc.vector.memset(conv_a[:, :, 0:PAD], 0.0))
                dve.wait_ge(conv_gate.sem, conv_gate(1))
                step(dve, nc.vector.tensor_tensor(conv_a[:, :, PAD:], conv_a[:, :, PAD:], conv_y[:, :, :], ALU.mult))
                for tap in range(31):
                    for f in range(4):
                        src = conv_a[:, f, tap:tap + SEQ]
                        if tap == 0:
                            ins = nc.vector.tensor_scalar(conv_y[:, f, :], src, cwT[:, f, 0:1], cb[:, f:f + 1], ALU.mult, ALU.add)
                        else:
                            ins = nc.vector.scalar_tensor_tensor(conv_y[:, f, :], src, cwT[:, f, tap:tap + 1], conv_y[:, f, :], ALU.mult, ALU.add)
                    step(dve, ins)
                mean_squares(kit, dve, sq, ms[:, 0:n_first], parts)
                dve.sem_inc(sums.sem, 1)
                dve.wait_ge(roots.sem, roots(1))
                scale_rows(kit, dve, ms[:, 0:n_first], parts)
                for t in range(TX):
                    v = heads(tb[:, t, DQ:DQ + 512])
                    rope(kit, dve, sq, v[:, :, 0:8], v[:, :, 8:16], kit.part("r8c", TX)[:, t, :], kit.part("r8s", TX)[:, t, :])
                    v = kd[:, t, :, :, 0, :].rearrange("p k g d -> p (k g) d")
                    rope(kit, dve, sq, v[:, :, 0:8], v[:, :, 8:16], kit.part("r8c", TX)[:, t, :], kit.part("r8s", TX)[:, t, :])
                    step(dve, nc.vector.tensor_copy(kd[:, t, :, :, 1, :].rearrange("p k g d -> p (k g) d"), v))
                dve.wait_ge(kv_ready.sem, kv_ready(1))
                n = N_CMP
                step(dve, nc.vector.tensor_copy(ck, kit.ps[0:n, 4, 0:128].rearrange("p (g d) -> p g d", g=2)))
                mean_squares(kit, dve, sq, ms[:, n_first:], cmp_parts)
                dve.sem_inc(sums.sem, 1)
                dve.wait_ge(roots.sem, roots(2))
                scale_rows(kit, dve, ms[:, n_first:], cmp_parts)
                rope(kit, dve, sq, ck[:, :, 0:8], ck[:, :, 8:16], kit.part("endc")[0:n, :], kit.part("ends")[0:n, :])
                step(dve, nc.vector.tensor_copy(kcd[0:n, :, 1, :], ck))
                dve.wait_ge(kv_ready.sem, kv_ready(2))
                step(dve, nc.vector.tensor_copy(vc[0:n, :, :], kit.ps[0:n, 5, 0:128].rearrange("p (g d) -> p g d", g=2)))

            def scalar(act):
                nc.scalar.activation(conv_y[:, :, :], conv_y[:, :, :], ACT.Sigmoid).then_inc(conv_gate.sem, 1)
                kit.act_step(act, nc.scalar.activation(tb[:, :, BGT:BGT + 24], tb[:, :, BGT:BGT + 24], ACT.Sigmoid))
                for i in range(2):
                    act.wait_ge(hid_sum.sem, hid_sum(i + 1))
                    nc.scalar.activation(hid[:, i, :].rearrange("p (g n) -> p g n", g=2), kit.ps[:, 2 * i:2 * i + 2, 0:N_CMP], ACT.Silu).then_inc(hid_ready.sem, 1)
                for i, part in enumerate((ms[:, 0:n_first], ms[0:N_CMP, n_first:])):
                    act.wait_ge(sums.sem, sums(i + 1))
                    root(kit, part).then_inc(roots.sem, 1)
                for n0, nn in ((CG, 512), (DG, 512), (MG, 256)):
                    kit.act_step(act, nc.scalar.activation(tb[:, :, n0:n0 + nn], tb[:, :, n0:n0 + nn], ACT.Silu))

            def tensor(pe):
                for i, name in enumerate(("cmp_k", "cmp_v")):
                    stream.arrived(pe, m[name])
                    w = stream.ring[:, m[name] % SLOTS, :].rearrange("p (l n) -> p l n", l=CMP_BLOCK)
                    pe.wait_ge(blocks_ready.sem, blocks_ready(i + 1))
                    for l in range(CMP_BLOCK):
                        for g in range(2):
                            ins = nc.tensor.matmul(kit.ps[:, 2 * i + g, 0:N_CMP], w[64 * g:64 * g + 64, l, :], blk[64 * g:64 * g + 64, i, l, :],
                                                   start=(l == 0), stop=(l == CMP_BLOCK - 1))
                    ins.then_inc(hid_sum.sem, 1)
                    pe.wait_ge(hid_sum.sem, hid_sum(i + 1))
                    pe.sem_inc(stream.used, 1)
                for i in range(2):
                    pe.wait_ge(hid_ready.sem, hid_ready(i + 1))
                    for g in range(2):
                        ins = nc.tensor.matmul(kit.ps[0:N_CMP, 4 + i, g * 64:(g + 1) * 64], hid[:, i, g * N_CMP:(g + 1) * N_CMP], w2[:, i, :], start=True, stop=True)
                    ins.then_inc(kv_ready.sem, 1)

            def sync(sp):
                stream.load_ahead(sp, m["cmp_v"] + 1)

            elementwise(kit, vector=vector, scalar=scalar, tensor=tensor, sync=sync)

        with ExitStack() as es:
            qT = kit.sb(es, "queries_turned", [P, 4, SEQ])
            kT = kit.sb(es, "keys_turned", [P, 2, 2, SEQ])
            kcT = kit.sb(es, "compressed_keys_turned", [P, 2, N_CMP])
            mqT = kit.sb(es, "mem_queries_turned", [P, 2, SEQ])
            mkT = kit.sb(es, "mem_keys_turned", [P, 2, MEM])
            o = kit.sb(es, "nsa_out", [P, TX, 512])
            gate = kit.sb(es, "gate_inv", [P, 2])
            yc = conv_a[:, :, 0:512]
            groups = []
            for dst, n0, nf in ((qT, DQ, 4), (mqT, MQ, 2)):
                for f in range(nf):
                    groups.append(([tb[:, t, n0 + f * P:n0 + (f + 1) * P] for t in range(TX)], dst[:, f, :].rearrange("p (t n) -> p t n", t=TX)))
            for kind in range(2):
                for g in range(2):
                    groups.append(([kd[:, t, kind, g, :, :].rearrange("p c d -> p (c d)") for t in range(TX)], kT[:, kind, g, :].rearrange("p (t n) -> p t n", t=TX)))
            for f in range(2):
                groups.append(([mem_kv[:, t, f * P:(f + 1) * P] for t in range(TM)], mkT[:, f, :].rearrange("p (t n) -> p t n", t=TM)))
            groups.append(([kcd[0:N_CMP, g, :, :].rearrange("p c d -> p (c d)") for g in range(2)], kcT[:, :, :]))
            for t in range(TX):
                groups.append(([conv_y[:, f, t * P:(t + 1) * P] for f in range(4)], yc[:, t, :].rearrange("p (f n) -> p f n", f=4)))
            turn(kit, groups)

            units = []
            for h in range(8):
                g, b = h // 4, 64 * (h % 2)
                for t in range(TX):
                    q = qT[b:b + 64, h // 2, t * P:(t + 1) * P]
                    for branch in range(3):
                        def finish(dve, psum, inv, h=h, t=t, branch=branch):
                            dst = o[:, t, h * 64:(h + 1) * 64]
                            gcol = tb[:, t, BGT + 3 * h + branch:BGT + 3 * h + branch + 1]
                            if branch == 0:
                                return nc.vector.tensor_scalar(dst, psum, inv, gcol, ALU.mult, ALU.mult)
                            w = gate[:, branch - 1:branch]
                            step(dve, nc.vector.tensor_tensor(w, inv, gcol, ALU.mult))
                            return nc.vector.scalar_tensor_tensor(dst, psum, w, dst, ALU.mult, ALU.add)
                        if branch == 0:
                            units.append(dict(maps=[(q, kcT[b:b + 64, g, :])], n=N_CMP, finish=finish, values=[vc[0:N_CMP, g, :]],
                                              mask=(kit.part("cmp_add", TX)[:, t, :], kit.part("cmp_mul", TX)[:, t, :])))
                        else:
                            v0 = KV + 256 * (branch - 1) + 128 + 64 * g
                            units.append(dict(maps=[(q, kT[b:b + 64, branch - 1, g, 0:(t + 1) * P])], n=(t + 1) * P, causal=True, finish=finish,
                                              values=[tb[:, s, v0:v0 + 64] for s in range(t + 1)]))
            attend(kit, units, 64 ** -0.5)
            attend(kit, memory_attention_units(kit, mqT, mkT, mem_kv, tb[:, :, MQ:MQ + 256]), 64 ** -0.5)

            normed = kit.counter("conv_normed", TX)
            activated = kit.counter("conv_activated", TX)
            with ExitStack() as e2:
                sq = kit.sb(e2, "squares", [P, 1024])
                ms = kit.sb(e2, "mean_squares", [P, TX])
                sums = kit.counter("mean_squares_ready", 1)
                roots = kit.counter("roots_ready", 1)
                parts = [(yc[:, t, :].unsqueeze(1), yc[:, t, :].unsqueeze(1), cn[:, :]) for t in range(TX)]

                def gate_vector(dve):
                    mean_squares(kit, dve, sq, ms, parts)
                    dve.sem_inc(sums.sem, 1)
                    dve.wait_ge(roots.sem, roots(1))
                    scale_rows(kit, dve, ms, parts)
                    dve.sem_inc(normed.sem, TX)
                    step(dve, nc.vector.tensor_tensor(tb[:, :, DQ:DQ + 512], o[:, :, :], tb[:, :, DG:DG + 512], ALU.mult))
                    step(dve, nc.vector.tensor_tensor(tb[:, :, KV:KV + 256], tb[:, :, MQ:MQ + 256], tb[:, :, MG:MG + 256], ALU.mult))
                    for t in range(TX):
                        dve.wait_ge(activated.sem, activated(t + 1))
                        step(dve, nc.vector.tensor_tensor(tb[:, t, CG:CG + 512], tb[:, t, CG:CG + 512], yc[:, t, :], ALU.mult))

                def gate_scalar(act):
                    act.wait_ge(sums.sem, sums(1))
                    root(kit, ms[:, :]).then_inc(roots.sem, 1)
                    for t in range(TX):
                        act.wait_ge(normed.sem, normed(t + 1))
                        nc.scalar.activation(yc[:, t, :], yc[:, t, :], ACT.Silu).then_inc(activated.sem, 1)
                elementwise(kit, vector=gate_vector, scalar=gate_scalar)
        with ExitStack() as es:
            mixT = kit.sb(es, "mix_turned", [P, 10, SEQ])
            turn_mix(kit, tb[:, :, 0:1280], mixT)
            project(kit, stream, m["out1"], residual_units(kit, x, mixT), engines=1)


CTX = 256
TC = CTX // P
TA = TC + TX
HEADS = 8
DN_QKV = 3 * HEADS * P
OFF_Z = DN_QKV
OFF_SMALL = OFF_Z + HEADS * P
N_SMALL = 16 + 16 + 384 + 256 + 64
OFF_GATE = OFF_SMALL + N_SMALL
Q_RANK, KV_RANK, ROPE = 384, 256, 64
QK = P + ROPE
FF = 1408
NF = FF // P
SEG_C, SEG_X, PADDED = 2, 2 + CTX + 2, 2 + CTX + 2 + SEQ + 2


def load_matrices_second(stream, a):
    m = {}
    w = a["w_in_2"][0]
    ada = a["ada_w_2"][0]
    m["ada_first"] = Matrix(stream, ada, columns(0, 2048), KD)
    m["in_first"] = Matrix(stream, w, columns(0, DN_QKV) + columns(OFF_SMALL, OFF_GATE), KD)
    m["in_z"] = Matrix(stream, w, columns(OFF_Z, OFF_SMALL), KD)
    m["uq"] = Matrix(stream, a["w_uq_2"][0], columns(0, HEADS * QK), 3)
    m["ukv"] = Matrix(stream, a["w_ukv_2"][0], columns(0, HEADS * 256), 2)
    m["in_gate"] = Matrix(stream, w, columns(OFF_GATE, OFF_GATE + 2 * D), KD)
    m["out_a"] = Matrix(stream, a["w_out_a_2"][0], columns(0, D), KD)
    m["out_b"] = Matrix(stream, a["w_out_b_2"][0], columns(0, D), KD)
    m["ada_second"] = Matrix(stream, ada, columns(2048, 6144), KD)
    m["w_o"] = Matrix(stream, a["w_o_2"][0], columns(0, D), KD)
    m["experts"] = []
    for e in range(N_EXPERTS):
        up = []
        for n0, nn in columns(0, FF):
            up.append((n0, nn, stream.add(a["w_gate_2"][0, e][:, n0:n0 + nn], KD, nn), stream.add(a["w_up_2"][0, e][:, n0:n0 + nn], KD, nn)))
        down = []
        for k0 in range(0, NF, 4):
            kk = min(4, NF - k0)
            down.append((k0, kk, stream.add(a["w_down_2"][0, e][k0 * P:(k0 + kk) * P, :], kk, D)))
        m["experts"].append((up, down))
    return m


def store(kit, pairs):
    nc = kit.nc
    parked = kit.counter("parked", 16 * len(pairs))
    with nc.Block() as block:

        @block.sync
        def _(sp):
            for dst, src in pairs:
                sp.dma_start(dst, src).then_inc(parked.sem, 16)
            sp.wait_ge(parked.sem, parked(16 * len(pairs)))


def ada_units(kit, cs, crep, bias, cols, rows):
    nc = kit.nc

    def units(n0, nn):
        if n0 // D in (2, 5):
            i, at = n0 // D // 3, n0 % D

            def row_put(eng, act, psum):
                dst = rows[:, i, at:at + nn]
                return nc.vector.tensor_tensor(dst, dst, psum, ALU.add)
            return [(P, nn, lambda w, j, k: (crep[:, k, :], w[:, j, :]), row_put)]

        def unit(f):
            c = n0 // P + f

            def put(eng, act, psum):
                return nc.vector.tensor_scalar(cols[:, c, :], psum, bias[:, c:c + 1], None, ALU.add)
            return P, 2, lambda w, j, k: (w[:, j, f * P:(f + 1) * P], cs[:, k, :]), put
        return [unit(f) for f in range(nn // P)]
    return units


def second_block(kit, stream, m, a, x, out, place, place3):
    nc = kit.nc
    step = kit.dve_step
    with ExitStack() as st:
        sb = lambda name, shape: kit.sb(st, name, shape)
        const = kit.place_constants(st, "constants2", place)
        x_park = nc.dram_tensor("x_park", (P, TX, D), F32).ap()
        h_park = nc.dram_tensor("h_park", (P, KD, SEQ), F32).ap()
        s_park = nc.dram_tensor("small_park", (P, TA, N_SMALL), F32).ap()
        y_park = nc.dram_tensor("y_park", (P, TX, D), F32).ap()
        cs = sb("silu_c", [P, KD, 2])
        ada_b = sb("ada_bias", [P, 48])
        cols = sb("modulation", [P, 48, 2])
        g12 = sb("norm_gains", [P, 2, KD])
        gx = sb("modulated_gain", [P, 3, KD])
        load(kit, [(const[:, :], a["constants2"]), (cs[:, :, 0], as_columns(a["c_2"][0])), (cs[:, :, 1], as_columns(a["c_ctx_2"])),
                   (ada_b[:, :], as_columns(a["ada_b_2"][0])), (g12[:, 0, :], as_columns(a["norm1_g_2"][0])), (g12[:, 1, :], as_columns(a["norm2_g_2"][0]))])
        elementwise(kit, scalar=lambda act: kit.act_step(act, nc.scalar.activation(cs[:, :, :], cs[:, :, :], ACT.Silu)))
        project(kit, stream, m["ada_first"], ada_units(kit, cs, None, ada_b, cols, None), engines=1)

        def gains(dve):
            for i in range(2):
                step(dve, nc.vector.scalar_tensor_tensor(gx[:, i, :], cols[:, 8:16, i], 1.0, g12[:, 0, :], ALU.add, ALU.mult))
        elementwise(kit, vector=gains)

        qk = sb("qk", [P, 2 * HEADS, PADDED])
        ab = sb("alpha_beta", [P, TA, 32])
        raw_v = sb("v_channels", [P, HEADS, PADDED])
        with ExitStack() as s2:
            with ExitStack() as hs:
                small = kit.sb(hs, "small", [P, TA, N_SMALL])
                hT = kit.sb(hs, "rows_turned", [P, KD, CTX + SEQ])
                norm_and_turn(kit, x, list(range(TX)), hT[:, :, CTX:], gx[:, 0, :], cols[:, 0:8, 0])
                store(kit, [(x_park, x[:, :, :]), (h_park, hT[:, :, CTX:])])
                load(kit, [(x[:, 0:TC, :], a["ctx_2"][0].rearrange("(t p) d -> p t d", p=P))])
                norm_and_turn(kit, x, list(range(TC)), hT[:, :, 0:CTX], gx[:, 1, :], cols[:, 0:8, 1])

                def units(n0, nn):
                    if n0 >= DN_QKV:
                        return by_tokens(kit, hT, range(TA), lambda t, n0, nn: small[:, t, n0 - OFF_SMALL:n0 - OFF_SMALL + nn])(n0, nn)

                    def unit(f, h0, n, seg):
                        c = n0 // P + f
                        dst = (qk[:, c, seg:seg + n] if c < 16 else raw_v[:, c - 16, seg:seg + n])
                        return P, n, lambda w, j, k: (w[:, j, f * P:(f + 1) * P], hT[:, k, h0:h0 + n]), put_copy(kit, dst)
                    return [u for f in range(nn // P) for u in (unit(f, 0, CTX, SEG_C), unit(f, CTX, SEQ, SEG_X))]
                project(kit, stream, m["in_first"], units, ahead=0)
                elementwise(kit, vector=lambda dve: step(dve, nc.vector.tensor_copy(ab[:, :, :], small[:, :, 0:32])))
                store(kit, [(s_park, small[:, :, :])])
            short_conv(kit, a, qk, raw_v)
            v_tok = kit.sb(s2, "v", [P, TA, HEADS * P])
            groups = []
            for t in range(TA):
                at = SEG_C + t * P if t < TC else SEG_X + (t - TC) * P
                for h0 in (0, 4):
                    groups.append(([raw_v[:, h, at:at + P] for h in range(h0, h0 + 4)], v_tok[:, t, h0 * P:(h0 + 4) * P].rearrange("p (h d) -> p h d", h=4)))
            turn(kit, groups)
            delta_net(kit, a, qk, v_tok, ab, (raw_v, stream.ring), x)
    with ExitStack() as st:
        second_half(kit, stream, m, a, x, out, place3, (x_park, h_park, s_park, y_park))


def short_conv(kit, a, qk, raw_v):
    nc = kit.nc
    step = kit.dve_step
    NT = 3 * HEADS
    L = PADDED - 4
    with ExitStack() as st:
        cw = kit.sb(st, "conv_w", [5, DN_QKV])
        cwT = kit.sb(st, "conv_w_turned", [P, NT, 5])
        y = kit.sb(st, "conv_out", [P, 2, L])
        sq = kit.sb(st, "conv_squares", [P, 2, L])
        load(kit, [(cw[:, :], a["conv_w_2"][0])])
        turn(kit, [([cw[:, f * P:(f + 1) * P] for f in range(f0, f0 + 4)], cwT[:, f0:f0 + 4, :]) for f0 in range(0, NT, 4)])

        def pads(dve):
            for buf in (qk, raw_v):
                for at in (0, 2 + CTX, PADDED - 2):
                    ins = nc.vector.memset(buf[:, :, at:at + 2], 0.0)
            step(dve, ins)
        elementwise(kit, vector=pads)

        def tile(c):
            return qk[:, c, :] if c < 16 else raw_v[:, c - 16, :]

        conv_ready = kit.counter("conv_ready", NT)
        silu_ready = kit.counter("silu_ready", NT)
        squared = kit.counter("squares_ready", 16)
        lengths = kit.counter("length_sums", 16)
        rooted = kit.counter("lengths_ready", 16)

        def vector(dve):
            def scale(c):
                dve.wait_ge(rooted.sem, rooted(c + 1))
                s = sq[:, c % 2, :]
                step(dve, nc.vector.reciprocal(s, s))
                d = tile(c)[:, 2:2 + L]
                if c < HEADS:
                    step(dve, nc.vector.scalar_tensor_tensor(d, d, P ** -0.5, s, ALU.mult, ALU.mult))
                else:
                    step(dve, nc.vector.tensor_tensor(d, d, s, ALU.mult))
            for c in range(NT):
                if c >= 2:
                    dve.wait_ge(silu_ready.sem, silu_ready(c - 1))
                d = y[:, c % 2, :]
                for tap in range(5):
                    src = tile(c)[:, tap:tap + L]
                    if tap == 0:
                        ins = nc.vector.tensor_scalar(d, src, cwT[:, c, 0:1], None, ALU.mult)
                    else:
                        ins = nc.vector.scalar_tensor_tensor(d, src, cwT[:, c, tap:tap + 1], d, ALU.mult, ALU.add)
                    if tap < 4:
                        step(dve, ins)
                ins.then_inc(conv_ready.sem, 1)
                if 1 <= c <= 16:
                    scale(c - 1)

        def scalar(act):
            for c in range(NT):
                act.wait_ge(conv_ready.sem, conv_ready(c + 1))
                nc.scalar.activation(tile(c)[:, 2:2 + L], y[:, c % 2, :], ACT.Silu).then_inc(silu_ready.sem, 1)
                if c < 16:
                    act.wait_ge(silu_ready.sem, silu_ready(c + 1))
                    if c >= 2:
                        act.wait_ge(kit.dve_step.sem, scaled_at(c - 2))
                    nc.scalar.activation(sq[:, c % 2, :], tile(c)[:, 2:2 + L], ACT.Square).then_inc(squared.sem, 1)
                    act.wait_ge(lengths.sem, lengths(c + 1))
                    nc.scalar.activation(sq[:, c % 2, :].rearrange("p (b n) -> p b n", b=2), kit.ps[:, 2 * (c % 2):2 * (c % 2) + 2, 0:L // 2],
                                         ACT.Sqrt, bias=kit.eps).then_inc(rooted.sem, 1)

        first = step.count

        def scaled_at(c):
            return first + 4 * (c + 2) + 2 * (c + 1)

        def tensor(pe):
            for c in range(16):
                pe.wait_ge(squared.sem, squared(c + 1))
                if c >= 2:
                    pe.wait_ge(rooted.sem, rooted(c - 1))
                for b in range(2):
                    ins = nc.tensor.matmul(kit.ps[:, 2 * (c % 2) + b, 0:L // 2], kit.part("ones"), sq[:, c % 2, b * (L // 2):(b + 1) * (L // 2)],
                                           start=True, stop=True)
                ins.then_inc(lengths.sem, 1)
        elementwise(kit, vector=vector, scalar=scalar, tensor=tensor)


def delta_net(kit, a, qk, v_tok, ab, scratch, o):
    nc = kit.nc
    step = kit.dve_step
    H = HEADS
    with ExitStack() as st:
        sb = lambda name, shape: kit.sb(st, name, shape)
        al = sb("minus_exp_a", [P, 16])
        dt = sb("dt_bias", [P, 16])
        z = sb("softplus_in", [P, TA, 16])
        e = sb("softplus_exp", [P, TA, 16])
        load(kit, [(al[:, :], row_bc(a["a_log_2"][0].rearrange("r h -> (r h)"))), (dt[:, :], row_bc(a["dt_bias_2"][0].rearrange("r h -> (r h)")))])
        g = sb("log_decay", [P, 2, TA, H])
        beta = sb("beta", [P, 2, TA, H])
        cum = sb("cum", [P, 2, TA, H])
        eg = sb("exp_cum", [P, 2, TA, H])
        egl = sb("exp_rest", [P, 2, TA, H])
        beg = sb("beta_exp_cum", [P, 2, TA, H])
        chunk_decay = sb("chunk_decay", [P, 2, 2, TA, H])
        asked = kit.counter("softplus_asked", 3)
        given = kit.counter("softplus_given", 3)
        summed = kit.counter("cum_summed", 1)
        W = 2 * TA * H

        def flat(v):
            return v[:, :, :, :].rearrange("p r t h -> p (r t h)")

        def vector(dve):
            step(dve, nc.vector.tensor_tensor(z[:, :, :], ab[:, :, 0:16], dt[:, :].unsqueeze(1).broadcast_to([P, TA, 16]), ALU.add))
            step(dve, nc.vector.tensor_scalar(e[:, :, :], z[:, :, :], -1.0, None, ALU.mult))
            step(dve, nc.vector.tensor_tensor(e[:, :, :], e[:, :, :], z[:, :, :], ALU.min))
            dve.sem_inc(asked.sem, 1)
            dve.wait_ge(given.sem, given(1))
            step(dve, nc.vector.scalar_tensor_tensor(z[:, :, :], z[:, :, :], 0.0, e[:, :, :], ALU.max, ALU.add))
            for r in range(2):
                step(dve, nc.vector.scalar_tensor_tensor(g[:, r, :, :], z[:, :, 8 * r:8 * r + 8], -1.0, al[:, 8 * r:8 * r + 8].unsqueeze(1).broadcast_to([P, TA, 8]), ALU.mult, ALU.mult))
            dve.sem_inc(asked.sem, 1)
            dve.wait_ge(summed.sem, summed(1))
            step(dve, nc.vector.tensor_copy(flat(cum), kit.ps[:, 0, 0:W]))
            step(dve, nc.vector.tensor_tensor(flat(egl), kit.ps[:, 1, 0:W], flat(cum), ALU.subtract))
            dve.sem_inc(asked.sem, 1)
            dve.wait_ge(given.sem, given(3))
            step(dve, nc.vector.tensor_tensor(flat(beg), flat(beta), flat(eg), ALU.mult))

        def scalar(act):
            astep = kit.act_step
            for r in range(2):
                astep(act, nc.scalar.activation(beta[:, r, :, :], ab[:, :, 16 + 8 * r:24 + 8 * r], ACT.Sigmoid))
            astep(act, nc.scalar.activation(al[:, :], al[:, :], ACT.Exp))
            act.wait_ge(asked.sem, asked(1))
            astep(act, nc.scalar.activation(e[:, :, :], e[:, :, :], ACT.Exp))
            nc.scalar.activation(e[:, :, :], e[:, :, :], ACT.Ln, bias=1.0).then_inc(given.sem, 1)
            act.wait_ge(asked.sem, asked(3))
            astep(act, nc.scalar.activation(flat(eg), flat(cum), ACT.Exp))
            nc.scalar.activation(flat(egl), flat(egl), ACT.Exp).then_inc(given.sem, 1)
            nc.scalar.activation(chunk_decay[:, :, :, :, :].rearrange("p a r t h -> p a (r t h)"), kit.ps[:, 2:4, 0:W], ACT.Exp).then_inc(given.sem, 1)

        def tensor(pe):
            pe.wait_ge(asked.sem, asked(2))
            for r, d in enumerate("fb"):
                nc.tensor.matmul(kit.ps[:, 0, r * TA * H:(r + 1) * TA * H], kit.part("tri_" + d), g[:, r, :, :].rearrange("p t h -> p (t h)"), start=True, stop=True)
            for b, name in ((1, "same"), (2, "half0"), (3, "half1")):
                ins = nc.tensor.matmul(kit.ps[:, b, 0:W], kit.part(name), flat(g), start=True, stop=True)
            ins.then_inc(summed.sem, 1)
        elementwise(kit, vector=vector, scalar=scalar, tensor=tensor)

        names = ("k_rows", "cum_rows", "decay", "m_all", "m_level", "t_inv", "t_inv_turned", "z_level",
                 "v_beta", "k_beta", "k_rest", "u", "w_turned", "qk_turned", "q_decayed", "state")
        bufs = []
        for room in scratch:
            flat_room = room[:, :, :].rearrange("p h n -> p (h n)")
            bufs += [flat_room[:, i * 512:(i + 1) * 512].rearrange("p (h n) -> p h n", h=4) for i in range(flat_room.shape[1] // 512)]
        chains = []
        for hg in range(2):
            T = {n: bufs.pop() if bufs else sb(n, [P, 4, P])[:, :, :] for n in names}
            chains.append((T, sb("v_new", [P, 2, 4, P])))

        def zero(dve):
            for _, v_new in chains:
                step(dve, nc.vector.memset(v_new[:, :, :, :], 0.0))
        elementwise(kit, vector=zero)

        batches = []
        for r in range(2):
            order = list(range(TA)) if r == 0 else list(range(TC - 1, -1, -1)) + list(range(TA - 1, TC - 1, -1))
            for i, t in enumerate(order):
                batches.append((r, t, i == 0))
        N = len(batches)
        LEVELS = [2, 4, 8, 16, 32]

        def at(t):
            return SEG_C + t * P if t < TC else SEG_X + (t - TC) * P

        def mask4(name):
            return kit.part(name).unsqueeze(1).broadcast_to([P, 4, P])

        def halves(r):
            return (0, 1) if r == 0 else (1, 0)

        def chain(hg):
            T, v_new = chains[hg]
            S = T["state"]
            sig = lambda n, c=1: kit.counter(f"{n}_{hg}", c * N)
            k_turned, trig_ready, cum_ready, prods, shifted, exps, m_ready, t_turned, t_ready = (
                sig(n) for n in ("k_turned", "trig_ready", "cum_rows_ready", "kk_ready", "shifted", "decays_ready", "m_ready", "t_turned", "t_ready"))
            masked, z_sum, z_ready, d_sum, t_next = (sig(n, 5) for n in ("level_masked", "z_summed", "z_ready", "d_summed", "t_next"))
            t_last = sig("t_last")
            k_ready, rows_ready, uw_sum, uw_ready = (sig(n) for n in ("k_rows_ready", "rows_ready", "uw_summed", "uw_ready"))
            ws_sum, vn_ready, os_sum, s_ready = (sig(n, 2) for n in ("ws_summed", "v_new_ready", "os_summed", "state_ready"))

            def bc(v, r, t):
                return v[:, r, t, 4 * hg:4 * hg + 4].unsqueeze(2).broadcast_to([P, 4, P])

            def bank(b):
                return kit.ps[:, 4 * hg + b, :].rearrange("p (h n) -> p h n", h=4)

            def run_tensor(pe):
                for b, (r, t, new) in enumerate(batches):
                    kt = [qk[:, 8 + 4 * hg + h, at(t):at(t) + P] for h in range(4)]
                    qt = [qk[:, 4 * hg + h, at(t):at(t) + P] for h in range(4)]
                    if b:
                        pe.wait_ge(uw_ready.sem, uw_ready(b))
                        pe.wait_ge(s_ready.sem, s_ready(2 * b))
                    for h in range(4):
                        ins = nc.tensor.transpose(bank(0)[:, h, :], kt[h], kit.ident)
                    ins.then_inc(k_turned.sem, 1)
                    for h in range(4):
                        nc.tensor.matmul(bank(2)[:, h, :], kt[h], kt[h], start=True, stop=True)
                        ins = nc.tensor.matmul(bank(3)[:, h, :], kt[h], qt[h], start=True, stop=True)
                    ins.then_inc(prods.sem, 1)
                    pe.wait_ge(trig_ready.sem, trig_ready(b + 1))
                    nc.tensor.matmul(kit.ps[:, 4 * hg + 1, :], kit.part("ones"), T["cum_rows"].rearrange("p h n -> p (h n)"), start=True, stop=True).then_inc(cum_ready.sem, 1)
                    yield
                    yield
                    pe.wait_ge(k_ready.sem, k_ready(b + 1))
                    pe.wait_ge(t_ready.sem, t_ready(b + 1))
                    for h in range(4):
                        ins = nc.tensor.transpose(bank(0)[:, h, :], T["t_inv"][:, h, :], kit.ident)
                    ins.then_inc(t_turned.sem, 1)
                    yield
                    for i, s in enumerate(LEVELS):
                        n = 5 * b + i
                        pe.wait_ge(masked.sem, masked(n + 1))
                        pe.wait_ge(t_next.sem, t_next(n + 1))
                        for h in range(4):
                            ins = nc.tensor.matmul(bank(0)[:, h, :], T["m_level"][:, h, :], T["t_inv_turned"][:, h, :], start=True, stop=True)
                        ins.then_inc(z_sum.sem, 1)
                        yield
                        pe.wait_ge(z_ready.sem, z_ready(n + 1))
                        for h in range(4):
                            nc.tensor.matmul(bank(1)[:, h, :], T["z_level"][:, h, :], T["t_inv"][:, h, :], start=True, stop=True)
                            ins = nc.tensor.matmul(bank(2)[:, h, :], T["t_inv"][:, h, :], T["z_level"][:, h, :], start=True, stop=True)
                        ins.then_inc(d_sum.sem, 1)
                        yield
                    pe.wait_ge(rows_ready.sem, rows_ready(b + 1))
                    pe.wait_ge(t_last.sem, t_last(b + 1))
                    for h in range(4):
                        nc.tensor.matmul(bank(1)[:, h, :], T["t_inv_turned"][:, h, :], T["v_beta"][:, h, :], start=True, stop=True)
                        ins = nc.tensor.matmul(bank(2)[:, h, :], T["k_beta"][:, h, :], T["t_inv_turned"][:, h, :], start=True, stop=True)
                    ins.then_inc(uw_sum.sem, 1)
                    yield
                    pe.wait_ge(uw_ready.sem, uw_ready(b + 1))
                    for i, half in enumerate(halves(r)):
                        n = 2 * b + i
                        lo, hi = 64 * half, 64 * half + 64
                        if n:
                            pe.wait_ge(s_ready.sem, s_ready(n))
                        for h in range(4):
                            ins = nc.tensor.matmul(bank(1)[lo:hi, h, :], T["w_turned"][:, h, lo:hi], S[:, h, :], start=True, stop=True)
                        ins.then_inc(ws_sum.sem, 1)
                        yield
                        pe.wait_ge(vn_ready.sem, vn_ready(n + 1))
                        for h in range(4):
                            if t >= TC:
                                nc.tensor.matmul(bank(3)[lo:hi, h, :], T["q_decayed"][:, h, lo:hi], S[:, h, :], start=True, stop=False)
                                nc.tensor.matmul(bank(3)[lo:hi, h, :], T["qk_turned"][:, h, lo:hi], v_new[:, half, h, :], start=False, stop=True)
                            ins = nc.tensor.matmul(bank(0)[:, h, :], T["k_rest"][:, h, :], v_new[:, half, h, :], start=True, stop=True)
                        ins.then_inc(os_sum.sem, 1)
                        yield

            def run_gpsimd(pool):
                for b, (r, t, new) in enumerate(batches):
                    d = "fb"[r]
                    if b:
                        pool.wait_ge(cum_ready.sem, cum_ready(b))
                    nc.gpsimd.tensor_tensor(T["cum_rows"], mask4("tri_" + d), bc(g, r, t), ALU.mult).then_inc(trig_ready.sem, 1)
                    yield
                    pool.wait_ge(m_ready.sem, m_ready(b + 1))
                    yield
                    for i, s in enumerate(LEVELS):
                        if i:
                            pool.wait_ge(z_sum.sem, z_sum(5 * b + i))
                        nc.gpsimd.tensor_tensor(T["m_level"], T["m_all"], mask4(f"level_{d}{s}"), ALU.mult).then_inc(masked.sem, 1)
                        if i == 1:
                            nc.gpsimd.tensor_tensor(T["v_beta"], v_tok[:, t, 512 * hg:512 * hg + 512].rearrange("p (h n) -> p h n", h=4), bc(beta, r, t), ALU.mult)
                        if i == 2:
                            pool.wait_ge(k_ready.sem, k_ready(b + 1))
                            nc.gpsimd.tensor_tensor(T["k_beta"], T["k_rows"], bc(beg, r, t), ALU.mult)
                        if i == 3:
                            nc.gpsimd.tensor_tensor(T["k_rest"], T["k_rows"], bc(egl, r, t), ALU.mult).then_inc(rows_ready.sem, 1)
                        yield
                        yield
                    for _ in range(6):
                        yield

            def run_scalar(act):
                for b, (r, t, new) in enumerate(batches):
                    act.wait_ge(k_turned.sem, k_turned(b + 1))
                    if b:
                        act.wait_ge(rows_ready.sem, rows_ready(b))
                    nc.scalar.activation(T["k_rows"], bank(0), ACT.Copy).then_inc(k_ready.sem, 1)
                    yield
                    act.wait_ge(shifted.sem, shifted(b + 1))
                    nc.scalar.activation(T["decay"], T["decay"], ACT.Exp)
                    nc.scalar.activation(T["q_decayed"], bank(1), ACT.Exp).then_inc(exps.sem, 1)
                    yield
                    yield
                    for i in range(5):
                        n = 5 * b + i
                        act.wait_ge(z_sum.sem, z_sum(n + 1))
                        if n:
                            act.wait_ge(d_sum.sem, d_sum(n))
                        nc.scalar.activation(T["z_level"], bank(0), ACT.Copy).then_inc(z_ready.sem, 1)
                        yield
                        yield
                    for _ in range(5):
                        yield

            def run_vector(dve):
                for b, (r, t, new) in enumerate(batches):
                    d = "fb"[r]
                    yield
                    dve.wait_ge(cum_ready.sem, cum_ready(b + 1))
                    step(dve, nc.vector.tensor_tensor(T["decay"], bank(1), bc(cum, r, t), ALU.subtract))
                    nc.vector.tensor_tensor(T["decay"], T["decay"], mask4("decay_t_" + d), ALU.subtract).then_inc(shifted.sem, 1)
                    dve.wait_ge(prods.sem, prods(b + 1))
                    step(dve, nc.vector.tensor_tensor(T["m_all"], bank(2), bc(beta, r, t), ALU.mult))
                    step(dve, nc.vector.tensor_tensor(T["t_inv"], T["m_all"], mask4(f"level_{d}1"), ALU.mult))
                    nc.vector.scalar_tensor_tensor(T["t_inv"], T["t_inv"], -1.0, mask4("ident"), ALU.mult, ALU.add).then_inc(t_ready.sem, 1)
                    dve.wait_ge(exps.sem, exps(b + 1))
                    nc.vector.tensor_tensor(T["qk_turned"], bank(3), T["decay"], ALU.mult)
                    qv = qk[:, 4 * hg:4 * hg + 4, at(t):at(t) + P]
                    nc.vector.tensor_tensor(T["q_decayed"], T["q_decayed"], qv, ALU.mult).then_inc(m_ready.sem, 1)
                    yield
                    dve.wait_ge(t_turned.sem, t_turned(b + 1))
                    nc.vector.tensor_copy(T["t_inv_turned"], bank(0)).then_inc(t_next.sem, 1)
                    yield
                    for i in range(5):
                        n = 5 * b + i
                        yield
                        dve.wait_ge(d_sum.sem, d_sum(n + 1))
                        tt = T["t_inv_turned"]
                        step(dve, nc.vector.tensor_tensor(T["t_inv"], T["t_inv"], bank(1), ALU.subtract))
                        ins = nc.vector.tensor_tensor(tt, tt, bank(2), ALU.subtract)
                        if i < 4:
                            ins.then_inc(t_next.sem, 1)
                        else:
                            step(dve, ins)
                            nc.vector.tensor_tensor(tt, tt, T["decay"], ALU.mult).then_inc(t_last.sem, 1)
                        yield
                    dve.wait_ge(uw_sum.sem, uw_sum(b + 1))
                    nc.vector.tensor_copy(T["u"], bank(1))
                    if new:
                        nc.vector.memset(S, 0.0)
                    nc.vector.tensor_copy(T["w_turned"], bank(2)).then_inc(uw_ready.sem, 1)
                    yield
                    for i, half in enumerate(halves(r)):
                        n = 2 * b + i
                        lo, hi = 64 * half, 64 * half + 64
                        dve.wait_ge(uw_ready.sem, uw_ready(b + 1))
                        dve.wait_ge(ws_sum.sem, ws_sum(n + 1))
                        nc.vector.tensor_tensor(v_new[lo:hi, half, :, :], T["u"][lo:hi], bank(1)[lo:hi], ALU.subtract).then_inc(vn_ready.sem, 1)
                        yield
                        dve.wait_ge(os_sum.sem, os_sum(n + 1))
                        if t >= TC:
                            dst = o[lo:hi, t - TC, 512 * hg:512 * hg + 512].rearrange("p (h n) -> p h n", h=4)
                            if r == 0:
                                ins = nc.vector.tensor_copy(dst, bank(3)[lo:hi])
                            else:
                                ins = nc.vector.tensor_tensor(dst, dst, bank(3)[lo:hi], ALU.add)
                            step(dve, ins)
                        a_c = chunk_decay[:, half, r, t, 4 * hg:4 * hg + 4].unsqueeze(2).broadcast_to([P, 4, P])
                        step(dve, nc.vector.tensor_tensor(S, S, a_c, ALU.mult))
                        nc.vector.tensor_tensor(S, S, bank(0), ALU.add).then_inc(s_ready.sem, 1)
                        yield
            return run_tensor, run_gpsimd, run_scalar, run_vector

        pair = [chain(hg) for hg in range(2)]

        def in_turn(engine_index):
            def program(eng):
                for _ in zip(pair[0][engine_index](eng), pair[1][engine_index](eng)):
                    pass
            return program
        elementwise(kit, tensor=in_turn(0), gpsimd=in_turn(1), scalar=in_turn(2), vector=in_turn(3))


def second_half(kit, stream, m, a, x, out, place, parked):
    nc = kit.nc
    step = kit.dve_step
    x_park, h_park, s_park, y_park = parked
    heads = lambda v, d: v.rearrange("p (h d) -> p h d", d=d)
    with ExitStack() as st:
        sb = lambda name, shape: kit.sb(st, name, shape)
        const = kit.place_constants(st, "constants3", place)
        cs = sb("silu_c", [P, KD, 2])
        ada_b = sb("ada_bias", [P, 48])
        cols = sb("modulation", [P, 48, 2])
        g2 = sb("norm2_gain", [P, KD])
        load(kit, [(const[:, :], a["constants3"]), (cs[:, :, 0], as_columns(a["c_2"][0])), (cs[:, :, 1], as_columns(a["c_ctx_2"])),
                   (ada_b[:, :], as_columns(a["ada_b_2"][0])), (g2[:, :], as_columns(a["norm2_g_2"][0]))])

        with ExitStack() as es:
            z = kit.sb(es, "z", [P, TX, D])
            gn = kit.sb(es, "dn_gain", [P, P])
            sq = kit.sb(es, "squares", [P, D])
            ms = kit.sb(es, "mean_squares", [P, TX * HEADS])
            hT = kit.sb(es, "rows_turned", [P, KD, SEQ])
            load(kit, [(gn[:, :], row_bc(a["dn_norm_g_2"][0])), (hT[:, :, :], h_park)])
            project(kit, stream, m["in_z"], by_tokens(kit, hT, range(TX), lambda t, n0, nn: z[:, t, n0 - OFF_Z:n0 - OFF_Z + nn]))
            sums = kit.counter("mean_squares_ready", 1)
            roots = kit.counter("roots_ready", 1)
            acts = kit.counter("activated", 1)
            parts = [(heads(x[:, t, :], P), heads(x[:, t, :], P), gn[:, :]) for t in range(TX)]

            def vector(dve):
                mean_squares(kit, dve, sq, ms, parts)
                dve.sem_inc(sums.sem, 1)
                dve.wait_ge(roots.sem, roots(1))
                scale_rows(kit, dve, ms, parts)
                dve.wait_ge(acts.sem, acts(1))
                step(dve, nc.vector.tensor_tensor(x[:, :, :], x[:, :, :], z[:, :, :], ALU.mult))

            def scalar(act):
                act.wait_ge(sums.sem, sums(1))
                root(kit, ms[:, :]).then_inc(roots.sem, 1)
                nc.scalar.activation(z[:, :, :], z[:, :, :], ACT.Silu).then_inc(acts.sem, 1)
            elementwise(kit, vector=vector, scalar=scalar)
            store(kit, [(y_park, x[:, :, :])])

        latent_attention(kit, stream, m, a, x, s_park)

        rows = sb("modulation_rows", [P, 2, D])

        with ExitStack() as es:
            gate = kit.sb(es, "branch_gates", [P, TX, 2 * D])
            yT = kit.sb(es, "branch_turned", [P, KD, SEQ])
            crep = kit.sb(es, "silu_c_repeated", [P, KD, P])
            hT = yT
            load(kit, [(hT[:, :, :], h_park)])
            project(kit, stream, m["in_gate"], by_tokens(kit, hT, range(TX), lambda t, n0, nn: gate[:, t, n0 - OFF_GATE:n0 - OFF_GATE + nn]))
            elementwise(kit, scalar=lambda act: kit.act_step(act, nc.scalar.activation(gate[:, :, :], gate[:, :, :], ACT.Sigmoid)))

            def gated(off):
                def units(n0, nn):
                    def unit(t):
                        def put(eng, act, psum):
                            dst = gate[:, t, off + n0:off + n0 + nn]
                            return nc.vector.tensor_tensor(dst, dst, psum, ALU.mult)
                        return P, nn, lambda w, j, k: (yT[:, k, t * P:(t + 1) * P], w[:, j, :]), put
                    return [unit(t) for t in range(TX)]
                return units
            with ExitStack() as e2:
                ya = kit.sb(e2, "y_a", [P, TX, D])
                load(kit, [(ya[:, :, :], y_park)])
                turn_mix(kit, ya, yT)
                project(kit, stream, m["out_a"], gated(0), engines=1)
                turn_mix(kit, x, yT)
                project(kit, stream, m["out_b"], gated(D), engines=1)
            elementwise(kit, vector=lambda dve: step(dve, nc.vector.tensor_tensor(gate[:, :, 0:D], gate[:, :, 0:D], gate[:, :, D:2 * D], ALU.add)))
            turn_mix(kit, gate[:, :, 0:D], yT)

            load(kit, [(x[:, :, :], x_park), (rows[:, 0, :], row_bc(a["ada_b_2"][0, 2 * D:3 * D])), (rows[:, 1, :], row_bc(a["ada_b_2"][0, 5 * D:6 * D]))])
            elementwise(kit, scalar=lambda act: kit.act_step(act, nc.scalar.activation(cs[:, :, :], cs[:, :, :], ACT.Silu)))
            elementwise(kit, vector=lambda dve: step(dve, nc.vector.tensor_copy(crep[:, :, :], cs[:, :, 0].unsqueeze(2).broadcast_to([P, KD, P]))))
            project(kit, stream, m["ada_second"], ada_units(kit, cs, crep, ada_b, cols, rows), engines=1)

            def out_units(n0, nn):
                def unit(t):
                    def put(eng, act, psum):
                        step(eng, nc.vector.tensor_tensor(psum, psum, rows[:, 0, n0:n0 + nn], ALU.mult))
                        dst = x[:, t, n0:n0 + nn]
                        return nc.vector.tensor_tensor(dst, dst, psum, ALU.add)
                    return P, nn, lambda w, j, k: (yT[:, k, t * P:(t + 1) * P], w[:, j, :]), put
                return [unit(t) for t in range(TX)]
            project(kit, stream, m["w_o"], out_units, engines=1)

        def gains(dve):
            step(dve, nc.vector.scalar_tensor_tensor(g2[:, :], cols[:, 32:40, 0], 1.0, g2[:, :], ALU.add, ALU.mult))
        elementwise(kit, vector=gains)
        hT = sb("h2_turned", [P, KD, SEQ])
        norm_and_turn(kit, x, list(range(TX)), hT, g2, cols[:, 24:32, 0])
        experts(kit, stream, m, a, x, hT, rows, out)


def latent_attention(kit, stream, m, a, x, s_park):
    nc = kit.nc
    step = kit.dve_step
    heads = lambda v, d: v.rearrange("p (h d) -> p h d", d=d)
    with ExitStack() as st:
        sb = lambda name, shape: kit.sb(st, name, shape)
        q = sb("queries", [P, TX, HEADS * QK])
        kv = sb("keys_values", [P, TA, HEADS * 256])
        kr = sb("key_rope", [P, TA, ROPE])
        gk = sb("key_gain", [P, QK])
        gq = sb("query_gain", [P, QK])
        sq = sb("squares", [P, HEADS * QK])
        ms = sb("mean_squares", [P, TX * HEADS + TA * HEADS + TA])
        NQ = TX * HEADS
        nope = lambda t: heads(kv[:, t, :], 256)[:, :, 0:P]
        load(kit, [(gk[:, :], row_bc(a["k_norm_g_2"][0])), (gq[:, :], row_bc(a["q_norm_g_2"][0]))])
        with ExitStack() as es:
            small = kit.sb(es, "small", [P, TA, N_SMALL])
            cqT = kit.sb(es, "c_q_turned", [P, 3, SEQ])
            ckvT = kit.sb(es, "c_kv_turned", [P, 2, CTX + SEQ])
            ga = kit.sb(es, "rank_gains", [P, Q_RANK + KV_RANK])
            load(kit, [(small[:, :, :], s_park), (ga[:, 0:Q_RANK], row_bc(a["q_a_norm_g_2"][0])), (ga[:, Q_RANK:], row_bc(a["kv_a_norm_g_2"][0]))])
            CQ, CKV, KR = 32, 32 + Q_RANK, 32 + Q_RANK + KV_RANK
            parts = []
            for t in range(TX):
                v = small[:, TC + t, CQ:CQ + Q_RANK].unsqueeze(1)
                parts.append((v, v, ga[:, 0:Q_RANK]))
            for t in range(TA):
                v = small[:, t, CKV:CKV + KV_RANK].unsqueeze(1)
                parts.append((v, v, ga[:, Q_RANK:]))
            sums = kit.counter("mean_squares_ready", 1)
            roots = kit.counter("roots_ready", 1)
            n = TX + TA

            def vector(dve):
                step(dve, nc.vector.tensor_copy(kr[:, :, :], small[:, :, KR:KR + ROPE]))
                mean_squares(kit, dve, sq, ms[:, 0:n], parts)
                dve.sem_inc(sums.sem, 1)
                dve.wait_ge(roots.sem, roots(1))
                scale_rows(kit, dve, ms[:, 0:n], parts)

            def scalar(act):
                act.wait_ge(sums.sem, sums(1))
                root(kit, ms[:, 0:n]).then_inc(roots.sem, 1)
            elementwise(kit, vector=vector, scalar=scalar)
            groups = []
            for f in range(3):
                groups.append(([small[:, TC + t, CQ + f * P:CQ + (f + 1) * P] for t in range(TX)], cqT[:, f, :].rearrange("p (t n) -> p t n", t=TX)))
            for f in range(2):
                for t0 in (0, 3):
                    groups.append(([small[:, t, CKV + f * P:CKV + (f + 1) * P] for t in range(t0, t0 + 3)],
                                   ckvT[:, f, t0 * P:(t0 + 3) * P].rearrange("p (t n) -> p t n", t=3)))
            turn(kit, groups)
            project(kit, stream, m["uq"], by_tokens(kit, cqT, range(TX), lambda t, n0, nn: q[:, t, n0:n0 + nn]))
            project(kit, stream, m["ukv"], by_tokens(kit, ckvT, range(TA), lambda t, n0, nn: kv[:, t, n0:n0 + nn]))

        q_parts = [(heads(q[:, t, :], QK), heads(q[:, t, :], QK), gq[:, :]) for t in range(TX)]
        kn_parts = [(nope(t), nope(t), gk[:, 0:P]) for t in range(TA)]
        kr_parts = [(kr[:, t, :].unsqueeze(1), None, None) for t in range(TA)]
        sums = kit.counter("mean_squares_ready", 1)
        roots = kit.counter("roots_ready", 1)
        msk = ms[:, NQ:NQ + TA * HEADS]
        msr = ms[:, NQ + TA * HEADS:]

        def vector(dve):
            mean_squares(kit, dve, sq, ms[:, 0:NQ], q_parts)
            mean_squares(kit, dve, sq, msk, kn_parts)
            mean_squares(kit, dve, sq, msr, kr_parts)
            step(dve, nc.vector.tensor_scalar(msr, msr, ROPE / QK, None, ALU.mult))
            r = msr.unsqueeze(2).broadcast_to([P, TA, HEADS])
            mk = msk.rearrange("p (t h) -> p t h", t=TA)
            step(dve, nc.vector.scalar_tensor_tensor(mk, mk, P / QK, r, ALU.mult, ALU.add))
            dve.sem_inc(sums.sem, 1)
            dve.wait_ge(roots.sem, roots(1))
            scale_rows(kit, dve, ms[:, 0:NQ], q_parts)
            scale_rows(kit, dve, msk, kn_parts)
            step(dve, nc.vector.tensor_tensor(kr[:, :, :], kr[:, :, :], gk[:, P:QK].unsqueeze(1).broadcast_to([P, TA, ROPE]), ALU.mult))
            for t in range(TX):
                for i, axis in enumerate(("row", "col")):
                    c, s = kit.part(axis + "c", TX)[:, t, :], kit.part(axis + "s", TX)[:, t, :]
                    v = heads(q[:, t, :], QK)
                    b = P + 32 * i
                    rope(kit, dve, sq, v[:, :, b:b + 16], v[:, :, b + 16:b + 32], c, s)
                    v = kr[:, TC + t, :].unsqueeze(1)
                    b = 32 * i
                    rope(kit, dve, sq, v[:, :, b:b + 16], v[:, :, b + 16:b + 32], c, s)

        def scalar(act):
            act.wait_ge(sums.sem, sums(1))
            root(kit, ms[:, 0:NQ + TA * HEADS]).then_inc(roots.sem, 1)
        elementwise(kit, vector=vector, scalar=scalar)

        HG = 2
        with ExitStack() as es:
            qn = kit.sb(es, "queries_turned", [P, HG, SEQ])
            qr = kit.sb(es, "query_ropes_turned", [ROPE, HG, SEQ])
            kn = kit.sb(es, "keys_turned", [P, HG, CTX + SEQ])
            krt = kit.sb(es, "key_ropes_turned", [ROPE, HG, CTX + SEQ])
            kh = kit.sb(es, "key_ropes", [P, TA, HG, ROPE])
            for h0 in range(0, HEADS, HG):
                def per_head(dve):
                    mk = msk.rearrange("p (t h) -> p t h", t=TA)
                    for t in range(TA):
                        r = mk[:, t, h0:h0 + HG].unsqueeze(2).broadcast_to([P, HG, ROPE])
                        ins = nc.vector.tensor_tensor(kh[:, t, :, :], kr[:, t, :].unsqueeze(1).broadcast_to([P, HG, ROPE]), r, ALU.mult)
                    step(dve, ins)
                elementwise(kit, vector=per_head)
                groups = []
                for i in range(HG):
                    h = h0 + i
                    for dst, src in ((qn, lambda t: q[:, t, h * QK:h * QK + P]), (qr, lambda t: q[:, t, h * QK + P:(h + 1) * QK])):
                        groups.append(([src(t) for t in range(TX)], dst[:, i, :].rearrange("p (t n) -> p t n", t=TX)))
                    for dst, src in ((kn, lambda t: kv[:, t, h * 256:h * 256 + P]), (krt, lambda t: kh[:, t, i, :])):
                        for t0 in (0, 3):
                            groups.append(([src(t) for t in range(t0, t0 + 3)], dst[:, i, t0 * P:(t0 + 3) * P].rearrange("p (t n) -> p t n", t=3)))
                turn(kit, groups)
                units = []
                for i in range(HG):
                    h = h0 + i
                    for t in range(TX):
                        def finish(dve, psum, inv, h=h, t=t):
                            return nc.vector.tensor_scalar(x[:, t, h * P:(h + 1) * P], psum, inv, None, ALU.mult)
                        units.append(dict(maps=[(qn[:, i, t * P:(t + 1) * P], kn[:, i, :])], more=(qr[:, i, t * P:(t + 1) * P], krt[:, i, :]), n=CTX + SEQ,
                                          values=[kv[:, s, h * 256 + P:(h + 1) * 256] for s in range(TA)], finish=finish))
                attend(kit, units, QK ** -0.5)


def experts(kit, stream, m, a, x, hT, rows, out):
    nc = kit.nc
    step = kit.dve_step
    E = N_EXPERTS
    SLOTS_ALL = E * CAP
    with ExitStack() as st:
        sb = lambda name, shape: kit.sb(st, name, shape)
        xe = sb("chosen_turned", [P, KD, SLOTS_ALL])
        back = sb("choice_turned", [P, E * CAP // P, SEQ])
        with ExitStack() as es:
            h2 = kit.sb(es, "h2_rows", [P, TX, D])
            rw = kit.sb(es, "router", [P, KD, E])
            aff = kit.sb(es, "affinity", [P, TX, E])
            mx = kit.sb(es, "affinity_max", [P, TX])
            affT = kit.sb(es, "affinity_turned", [E, SEQ])
            work = kit.sb(es, "affinity_left", [E, SEQ])
            top = kit.sb(es, "top8", [E, 8])
            sel = kit.sb(es, "chosen", [P, TX, E])
            slot = kit.sb(es, "slot", [P, TX, E])
            choice = kit.sb(es, "choice", [P, TX, SLOTS_ALL])
            load(kit, [(rw[:, :, :], a["router_w_2"][0].rearrange("(k p) e -> p k e", p=P))])
            turn(kit, [([hT[:, k, t * P:(t + 1) * P] for k in range(k0, k0 + 4)], h2[:, t, k0 * P:(k0 + 4) * P].rearrange("p (k n) -> p k n", k=4))
                       for t in range(TX) for k0 in (0, 4)])
            logits = kit.counter("logits", 1)
            shifted = kit.counter("logits_shifted", 1)
            exps = kit.counter("affinity_exps", 1)
            aff_ready = kit.counter("affinity_ready", 1)
            aff_turned = kit.counter("affinity_turned", 1)
            chosen = kit.counter("chosen_ready", 1)
            chosen_turned = kit.counter("chosen_turned", 1)
            chosen_rows = kit.counter("chosen_rows", 1)
            counted = kit.counter("slots_counted", 1)

            def tensor(pe):
                for t in range(TX):
                    for k in range(KD):
                        ins = nc.tensor.matmul(kit.ps[:, 0, t * E:(t + 1) * E], hT[:, k, t * P:(t + 1) * P], rw[:, k, :], start=(k == 0), stop=(k == KD - 1))
                ins.then_inc(logits.sem, 1)
                pe.wait_ge(aff_ready.sem, aff_ready(1))
                for t in range(TX):
                    ins = nc.tensor.transpose(kit.ps[0:E, 1, t * P:(t + 1) * P], aff[:, t, :], kit.ident)
                ins.then_inc(aff_turned.sem, 1)
                pe.wait_ge(chosen.sem, chosen(1))
                for t in range(TX):
                    ins = nc.tensor.transpose(kit.ps[:, 2, t * E:(t + 1) * E], work[:, t * P:(t + 1) * P], kit.ident[0:E, 0:E])
                ins.then_inc(chosen_turned.sem, 1)
                pe.wait_ge(chosen_rows.sem, chosen_rows(1))
                for t in range(TX):
                    for s in range(t + 1):
                        ins = nc.tensor.matmul(kit.ps[:, 3, t * E:(t + 1) * E], kit.part("upper" if s == t else "ones"), sel[:, s, :], start=(s == 0), stop=(s == t))
                ins.then_inc(counted.sem, 1)

            def scalar(act):
                act.wait_ge(shifted.sem, shifted(1))
                nc.scalar.activation(aff[:, :, :], aff[:, :, :], ACT.Exp).then_inc(exps.sem, 1)

            def vector(dve):
                bc = lambda v: v[:, :].unsqueeze(2).broadcast_to([P, TX, E])
                view = lambda b: kit.ps[:, b, 0:TX * E].rearrange("p (t e) -> p t e", t=TX)
                dve.wait_ge(logits.sem, logits(1))
                step(dve, nc.vector.tensor_reduce(mx[:, :], view(0), AX_X, ALU.max))
                step(dve, nc.vector.tensor_tensor(aff[:, :, :], view(0), bc(mx), ALU.subtract))
                dve.sem_inc(shifted.sem, 1)
                dve.wait_ge(exps.sem, exps(1))
                step(dve, nc.vector.tensor_reduce(mx[:, :], aff[:, :, :], AX_X, ALU.add))
                step(dve, nc.vector.reciprocal(mx[:, :], mx[:, :]))
                step(dve, nc.vector.tensor_tensor(aff[:, :, :], aff[:, :, :], bc(mx), ALU.mult))
                dve.sem_inc(aff_ready.sem, 1)
                dve.wait_ge(aff_turned.sem, aff_turned(1))
                step(dve, nc.vector.tensor_copy(affT[:, :], kit.ps[0:E, 1, :]))
                step(dve, nc.vector.tensor_copy(work[:, :], affT[:, :]))
                for _ in range(CAP // 8):
                    step(dve, nc.vector.max(top[:, :], work[:, :]))
                    step(dve, nc.vector.match_replace(work[:, :], top[:, :], work[:, :], -1.0))
                step(dve, nc.vector.tensor_tensor(work[:, :], work[:, :], affT[:, :], ALU.not_equal))
                dve.sem_inc(chosen.sem, 1)
                dve.wait_ge(chosen_turned.sem, chosen_turned(1))
                step(dve, nc.vector.tensor_copy(sel[:, :, :], view(2)))
                dve.sem_inc(chosen_rows.sem, 1)
                dve.wait_ge(counted.sem, counted(1))
                step(dve, nc.vector.tensor_tensor(slot[:, :, :], view(3), sel[:, :, :], ALU.mult))
                for t in range(TX):
                    c = choice[:, t, :].rearrange("p (e s) -> p e s", e=E)
                    ins = nc.vector.tensor_tensor(c, slot[:, t, :].unsqueeze(2).broadcast_to([P, E, CAP]),
                                                  kit.part("slot_iota").unsqueeze(1).broadcast_to([P, E, CAP]), ALU.is_equal)
                step(dve, ins)
            elementwise(kit, vector=vector, scalar=scalar, tensor=tensor)

            picked = kit.counter("picked", 2 * KD)
            kept = [kit.counter("taken_dve", KD), kit.counter("taken_act", KD)]

            def pick(pe):
                for u in range(2 * KD):
                    k, half = u // 2, u % 2
                    if u >= 8:
                        pe.wait_ge(kept[u % 2].sem, kept[u % 2]((u - 8) // 2 + 1))
                    for t in range(TX):
                        ins = nc.tensor.matmul(kit.ps[:, u % 8, :], h2[:, t, k * P:(k + 1) * P], choice[:, t, half * 512:(half + 1) * 512],
                                               start=(t == 0), stop=(t == TX - 1))
                    ins.then_inc(picked.sem, 1)

            def keep_even(dve):
                for u in range(0, 2 * KD, 2):
                    dve.wait_ge(picked.sem, picked(u + 1))
                    nc.vector.tensor_copy(xe[:, u // 2, 0:512], kit.ps[:, u % 8, :]).then_inc(kept[0].sem, 1)

            def keep_odd(act):
                for u in range(1, 2 * KD, 2):
                    act.wait_ge(picked.sem, picked(u + 1))
                    nc.scalar.activation(xe[:, u // 2, 512:1024], kit.ps[:, u % 8, :], ACT.Copy).then_inc(kept[1].sem, 1)
            elementwise(kit, vector=keep_even, scalar=keep_odd, tensor=pick)

            def weigh(dve):
                for t in range(TX):
                    c = choice[:, t, :].rearrange("p (e s) -> p e s", e=E)
                    ins = nc.vector.tensor_tensor(c, c, aff[:, t, :].unsqueeze(2).broadcast_to([P, E, CAP]), ALU.mult)
                step(dve, ins)
            elementwise(kit, vector=weigh)
            turn(kit, [([choice[:, t, k * P:(k + 1) * P] for t in range(TX)], back[:, k, :].rearrange("p (t n) -> p t n", t=TX))
                       for k in range(SLOTS_ALL // P)])

        ye = sb("expert_out", [P, SLOTS_ALL // P, D])
        with ExitStack() as es:
            hid = kit.sb(es, "hidden", [P, 2, FF])
            hidT = kit.sb(es, "hidden_turned", [P, 2, NF, CAP])
            G = 3 * E
            gate_up = kit.counter("gate_up", G)
            silu = kit.counter("gate_silu", G)
            hid_ready = kit.counter("hidden_ready", G)
            hid_turned = kit.counter("hidden_turned", 2 * E)
            hid_kept = kit.counter("hidden_kept", 2 * E)
            down_done = kit.counter("down_done", E)
            down_kept = kit.counter("down_kept", 2 * E)

            def rows_of(e):
                return slice(64 * (e % 2), 64 * (e % 2) + 64)

            def tensor(pe):
                def gates(e):
                    r = rows_of(e)
                    for i, (n0, nn, cg, cu) in enumerate(m["experts"][e][0]):
                        n = 3 * e + i
                        if n >= 2:
                            pe.wait_ge(hid_ready.sem, hid_ready(n - 1))
                        for c, bank in ((cg, 2 * (n % 2)), (cu, 2 * (n % 2) + 1)):
                            stream.arrived(pe, c)
                            w = stream.chunk(c)
                            for k in range(KD):
                                ins = nc.tensor.matmul(kit.ps[r, bank, 0:nn], xe[:, k, e * CAP:(e + 1) * CAP], w[:, k, :], start=(k == 0), stop=(k == KD - 1))
                            if bank % 2 == 0:
                                ins.then_inc(stream.used, 1)
                        ins.then_inc(gate_up.sem, 1)
                        pe.wait_ge(gate_up.sem, gate_up(n + 1))
                        pe.sem_inc(stream.used, 1)

                def down(e):
                    r = rows_of(e)
                    for half, (f0, f1) in enumerate(((0, 8), (8, NF))):
                        pe.wait_ge(hid_ready.sem, hid_ready(3 * e + (2 if half == 0 else 3)))
                        if e:
                            pe.wait_ge(hid_kept.sem, hid_kept(2 * e - 1 + half))
                        for f in range(f0, f1):
                            ins = nc.tensor.transpose(kit.ps[:, 4 + half, (f - f0) * 64:(f - f0) * 64 + 64], hid[r, e % 2, f * P:(f + 1) * P], kit.ident[r, r])
                        ins.then_inc(hid_turned.sem, 1)
                    if e:
                        pe.wait_ge(down_kept.sem, down_kept(2 * e))
                    pe.wait_ge(hid_kept.sem, hid_kept(2 * e + 2))
                    for k0, kk, c in m["experts"][e][1]:
                        stream.arrived(pe, c)
                        w = stream.chunk(c)
                        for j in range(kk):
                            for b in range(2):
                                ins = nc.tensor.matmul(kit.ps[r, 6 + b, :], hidT[:, e % 2, k0 + j, :], w[:, j, b * 512:(b + 1) * 512],
                                                       start=(k0 + j == 0), stop=(k0 + j == NF - 1))
                        if k0 + kk < NF:
                            ins.then_inc(stream.used, 1)
                    ins.then_inc(down_done.sem, 1)
                    pe.wait_ge(down_done.sem, down_done(e + 1))
                    pe.sem_inc(stream.used, 1)
                for e in range(E):
                    gates(e)
                    down(e)

            def scalar(act):
                for e in range(E):
                    r = rows_of(e)
                    for i, (n0, nn, _, _) in enumerate(m["experts"][e][0]):
                        n = 3 * e + i
                        act.wait_ge(gate_up.sem, gate_up(n + 1))
                        if e >= 2 and i == 0:
                            act.wait_ge(hid_turned.sem, hid_turned(2 * (e - 1)))
                        nc.scalar.activation(hid[r, e % 2, n0:n0 + nn], kit.ps[r, 2 * (n % 2), 0:nn], ACT.Silu).then_inc(silu.sem, 1)
                    for half, (f0, f1) in enumerate(((0, 8), (8, NF))):
                        act.wait_ge(hid_turned.sem, hid_turned(2 * e + half + 1))
                        if e >= 2:
                            act.wait_ge(down_done.sem, down_done(e - 1))
                        nc.scalar.activation(hidT[:, e % 2, f0:f1, :].rearrange("p f n -> p (f n)"), kit.ps[:, 4 + half, 0:(f1 - f0) * 64], ACT.Copy).then_inc(hid_kept.sem, 1)

            def vector(dve):
                def keep_down(e):
                    r = rows_of(e)
                    dve.wait_ge(down_done.sem, down_done(e + 1))
                    for b in range(2):
                        nc.vector.tensor_copy(ye[r, e // 2, b * 512:(b + 1) * 512], kit.ps[r, 6 + b, :]).then_inc(down_kept.sem, 1)
                for e in range(E):
                    r = rows_of(e)
                    for i, (n0, nn, _, _) in enumerate(m["experts"][e][0]):
                        n = 3 * e + i
                        dve.wait_ge(silu.sem, silu(n + 1))
                        h = hid[r, e % 2, n0:n0 + nn]
                        nc.vector.tensor_tensor(h, h, kit.ps[r, 2 * (n % 2) + 1, 0:nn], ALU.mult).then_inc(hid_ready.sem, 1)
                    keep_down(e)

            def sync(sp):
                stream.load_ahead(sp, len(stream.plan))
            elementwise(kit, vector=vector, scalar=scalar, tensor=tensor, sync=sync)

        combined = kit.counter("combined", 8)
        final = kit.counter("final_ready", 8)
        stored = kit.counter("stored", 16 * 8)

        def combine(pe):
            for u in range(8):
                t, b = u // 2, u % 2
                for k in range(SLOTS_ALL // P):
                    ins = nc.tensor.matmul(kit.ps[:, u, :], back[:, k, t * P:(t + 1) * P], ye[:, k, b * 512:(b + 1) * 512],
                                           start=(k == 0), stop=(k == SLOTS_ALL // P - 1))
                ins.then_inc(combined.sem, 1)

        def finish(dve):
            for u in range(8):
                t, b = u // 2, u % 2
                dve.wait_ge(combined.sem, combined(u + 1))
                psum = kit.ps[:, u, :]
                step(dve, nc.vector.tensor_tensor(psum, psum, rows[:, 1, b * 512:(b + 1) * 512], ALU.mult))
                dst = x[:, t, b * 512:(b + 1) * 512]
                nc.vector.tensor_tensor(dst, dst, psum, ALU.add).then_inc(final.sem, 1)

        def write(sp):
            for u in range(8):
                t, b = u // 2, u % 2
                sp.wait_ge(final.sem, final(u + 1))
                sp.dma_start(out[0, t * P:(t + 1) * P, b * 512:(b + 1) * 512], x[:, t, b * 512:(b + 1) * 512]).then_inc(stored.sem, 16)
            sp.wait_ge(stored.sem, stored(16 * 8))
        elementwise(kit, vector=finish, tensor=combine, sync=write)


NAMES = ["x", "mem", "mem_norm", "l0_norm", "l0_w_in", "l0_a_vnorm", "l0_a_ws", "l0_a_bs", "l0_b_qnorm", "l0_b_knorm",
         "l0_b_lq1", "l0_b_lk1", "l0_b_lq2", "l0_b_lk2", "l0_b_subln", "l0_m_wkv", "l0_m_qnorm", "l0_m_knorm",
         "l0_w_out", "l1_norm", "l1_w_in", "l1_c_conv_w", "l1_c_conv_b", "l1_c_norm", "l1_d_qnorm", "l1_d_knorm",
         "l1_d_cmp_pos_k", "l1_d_cmp_w1_k", "l1_d_cmp_w2_k", "l1_d_cmp_pos_v", "l1_d_cmp_w1_v", "l1_d_cmp_w2_v",
         "l1_m_wkv", "l1_m_qnorm", "l1_m_knorm", "l1_w_out", "c_2", "ctx_2", "c_ctx_2", "ada_w_2", "ada_b_2",
         "norm1_g_2", "norm2_g_2", "w_in_2", "conv_w_2", "a_log_2", "dt_bias_2", "dn_norm_g_2", "w_out_a_2",
         "q_a_norm_g_2", "w_uq_2", "kv_a_norm_g_2", "w_ukv_2", "q_norm_g_2", "k_norm_g_2", "w_out_b_2", "w_o_2",
         "router_w_2", "w_gate_2", "w_up_2", "w_down_2"]


def build(nc, a, places, out, stages=("first", "second")):
    with ExitStack() as stack:
        kit = Kit(nc, stack)
        const = kit.place_constants(stack, "constants", places[0])
        kit.minus_lam = kit.sb(stack, "minus_lambda", [P, 1])
        kit.ident = kit.part("ident")
        kit.eps = kit.part("eps")
        kit.causal = kit.part("causal")
        x = kit.sb(stack, "x", [P, TX, D])
        stream = WeightStream(kit, stack)
        m = {}
        if "first" in stages:
            m |= load_matrices_first(stream, a)
        if "second" in stages:
            m |= load_matrices_second(stream, a)
        load(kit, [(const[:, :], a["constants"]), (x[:, :, :], a["x"][0].rearrange("(t p) d -> p t d", p=P))])
        if "first" in stages:
            with ExitStack() as st:
                memT = kit.sb(st, "memory_turned", [P, KD, MEM])
                with ExitStack() as ms:
                    mem = kit.sb(ms, "memory", [P, TM, D])
                    g = kit.sb(ms, "memory_gain", [P, KD])
                    load(kit, [(mem[:, :, :], a["mem"][0].rearrange("(t p) d -> p t d", p=P)), (g[:, :], as_columns(a["mem_norm"]))])
                    norm_and_turn(kit, mem, list(range(TM)), memT, g)
                first_layer(kit, stream, m, a, x, memT)
                second_layer(kit, stream, m, a, x, memT)
        if "second" in stages:
            second_block(kit, stream, m, a, x, out, places[1], places[2])


def kernel(**inputs):
    import concourse.bacc as bacc
    from concourse.bass_utils import run_bass_kernel_spmd

    nc = bacc.Bacc("TRN2", target_bir_lowering=False, num_devices=1)
    const, place = constants(constant_parts())
    const2, place2 = constants(second_constant_parts())
    const3, place3 = constants(third_constant_parts())
    arrays = {f"in_{n}": np.ascontiguousarray(inputs[n]) for n in NAMES}
    arrays["in_constants"] = const
    arrays["in_constants2"] = const2
    arrays["in_constants3"] = const3
    args = {k[3:]: nc.dram_tensor(k, v.shape, mybir.dt.from_np(v.dtype), kind="ExternalInput").ap() for k, v in arrays.items()}
    out = nc.dram_tensor("out", (1, SEQ, D), F32, kind="ExternalOutput").ap()
    build(nc, args, (place, place2, place3), out)
    r = run_bass_kernel_spmd(nc, [arrays], core_ids=[0])
    return r.results[0]["out"]
```
